# Optimizing a Trainium2 kernel written in Bass

```python
import math
import jax, jax.numpy as jnp
from jax import lax
import numpy as np

D_MODEL = 1024
BATCH = 1
SEQ = 512
DEPTH = 1

MIX_WIDTH = D_MODEL
DIFF_WIDTH = MIX_WIDTH // 2
RET_WIDTH = MIX_WIDTH - DIFF_WIDTH
N_DIFF_HEADS = 4
DIFF_V_DIM = DIFF_WIDTH // N_DIFF_HEADS
DIFF_QK_DIM = DIFF_V_DIM // 2
N_RET_HEADS = 4
RET_V_DIM = RET_WIDTH // N_RET_HEADS
RET_QK_DIM = RET_V_DIM // 2
DIFF_QK_COLS = N_DIFF_HEADS * 2 * DIFF_QK_DIM
RET_QK_COLS = N_RET_HEADS * RET_QK_DIM
SPLIT_SIZES = (DIFF_QK_COLS, DIFF_QK_COLS, DIFF_WIDTH, RET_QK_COLS, RET_QK_COLS, RET_WIDTH, RET_WIDTH)
SPLIT_POINTS = (512, 1024, 1536, 1792, 2048, 2560)
IN_COLS = 3072

ROPE_THETA = 500000.0
ROPE_FRACTION = 4
RET_THETA = 10000.0
Q_BLOCK = 128
RET_CHUNK = 128

N_KEYS = 128
N_EXPERTS = N_KEYS * N_KEYS
PEER_HEADS = 8
PEER_TOPK = 16
PEER_KEY_DIM = 256
PEER_TOKEN_BLOCK = 128

EPS = 1e-6


def rmsnorm(x, g):
    x32 = x.astype(jnp.float32)
    y = x32 * lax.rsqrt(jnp.mean(x32 * x32, axis=-1, keepdims=True) + EPS)
    return (y * g.astype(jnp.float32)).astype(x.dtype)

def group_norm(o, g):
    mu = jnp.mean(o, axis=-1, keepdims=True)
    c = o - mu
    var = jnp.mean(c * c, axis=-1, keepdims=True)
    return c * lax.rsqrt(var + EPS) * g.astype(jnp.float32)

def rotate_prefix(x, pos, inv_freq):
    half = inv_freq.shape[0]
    rot = 2 * half
    ang = pos[:, None] * inv_freq[None, :]
    shape = (1, pos.shape[0]) + (1,) * (x.ndim - 3) + (half,)
    cos = jnp.cos(ang).reshape(shape)
    sin = jnp.sin(ang).reshape(shape)
    xf = x.astype(jnp.float32)
    x1 = xf[..., :half]
    x2 = xf[..., half:rot]
    out = jnp.concatenate([x1 * cos - x2 * sin, x2 * cos + x1 * sin, xf[..., rot:]], axis=-1)
    return out.astype(x.dtype)

def diff_attention(q, k, v, lam):
    B, S, H, _, d = q.shape
    nb = S // Q_BLOCK
    scale = d ** -0.5
    q_blocks = q.reshape(B, nb, Q_BLOCK, H, 2, d).transpose(1, 0, 2, 3, 4, 5)

    def one_block(qb):
        s = jnp.einsum('bqhmd,bkhmd->bhmqk', qb, k).astype(jnp.float32) * scale
        p = jax.nn.softmax(s, axis=-1)
        a = p[:, :, 0] - lam * p[:, :, 1]
        return jnp.einsum('bhqk,bkhe->bqhe', a.astype(v.dtype), v)

    o = lax.map(one_block, q_blocks)
    return o.transpose(1, 0, 2, 3, 4).reshape(B, S, H, v.shape[-1])

def retention_direction(q, k, v, log_gamma, strict):
    B, S, H, dk = q.shape
    dv = v.shape[-1]
    C = RET_CHUNK
    nc = S // C
    qc = q.reshape(B, nc, C, H, dk).transpose(1, 0, 3, 2, 4)
    kc = k.reshape(B, nc, C, H, dk).transpose(1, 0, 3, 2, 4)
    vc = v.reshape(B, nc, C, H, dv).transpose(1, 0, 3, 2, 4)
    idx = jnp.arange(C, dtype=jnp.float32)
    dist = idx[:, None] - idx[None, :]
    mask = (dist > 0) if strict else (dist >= 0)
    lg = log_gamma[:, None, None]
    decay_in = jnp.where(mask[None], jnp.exp(lg * jnp.maximum(dist, 0.0)[None]), 0.0)
    q_decay = jnp.exp(log_gamma[:, None] * (idx + 1.0)[None])[None, :, :, None]
    k_decay = jnp.exp(log_gamma[:, None] * (C - 1.0 - idx)[None])[None, :, :, None]
    chunk_decay = jnp.exp(log_gamma * C)[None, :, None, None]

    def step(state, inp):
        qi, ki, vi = inp
        inner = jnp.einsum('bhid,bhjd->bhij', qi, ki) * decay_in[None]
        o = jnp.einsum('bhij,bhjv->bhiv', inner, vi) + jnp.einsum('bhid,bhdv->bhiv', qi * q_decay, state)
        state = state * chunk_decay + jnp.einsum('bhjd,bhjv->bhdv', ki * k_decay, vi)
        return state, o

    state0 = jnp.zeros((B, H, dk, dv), jnp.float32)
    _, o = lax.scan(step, state0, (qc, kc, vc))
    return o.transpose(1, 0, 3, 2, 4).reshape(B, S, H, dv)

def peer_ffn(xn, w_query, sub_keys, expert_down, expert_up):
    B, S, D = xn.shape
    T = B * S
    nb = T // PEER_TOKEN_BLOCK
    x_blocks = xn.reshape(nb, PEER_TOKEN_BLOCK, D)

    def one_block(xb):
        tb = xb.shape[0]
        q = (xb @ w_query).reshape(tb, PEER_HEADS, 2, PEER_KEY_DIM // 2)
        s = jnp.einsum('thpd,hpnd->thpn', q, sub_keys).astype(jnp.float32)
        top_s, top_i = lax.top_k(s, PEER_TOPK)
        cand_s = (top_s[:, :, 0, :, None] + top_s[:, :, 1, None, :]).reshape(tb, PEER_HEADS, PEER_TOPK * PEER_TOPK)
        cand_i = (top_i[:, :, 0, :, None] * N_KEYS + top_i[:, :, 1, None, :]).reshape(tb, PEER_HEADS, PEER_TOPK * PEER_TOPK)
        best_s, pos = lax.top_k(cand_s, PEER_TOPK)
        eid = jnp.take_along_axis(cand_i, pos, axis=-1)
        gate = jax.nn.softmax(best_s, axis=-1)
        u = jnp.take(expert_down, eid, axis=0)
        act = jax.nn.gelu(jnp.einsum('thkd,td->thk', u, xb).astype(jnp.float32), approximate=False)
        v = jnp.take(expert_up, eid, axis=0)
        return jnp.einsum('thk,thkd->td', (gate * act).astype(v.dtype), v)

    out = lax.map(one_block, x_blocks)
    return out.reshape(B, S, D).astype(xn.dtype)

def first_inputs(seed: int = 0) -> dict:
    key = jax.random.key(seed)
    ks = jax.random.split(key, 16)
    f32 = jnp.float32
    nrm = jax.random.normal
    x = nrm(ks[0], (BATCH, SEQ, D_MODEL), f32)
    attn_norm_g = 1.0 + 0.02 * nrm(ks[1], (DEPTH, D_MODEL), f32)
    w_in = nrm(ks[2], (DEPTH, D_MODEL, IN_COLS), f32) * D_MODEL ** -0.5
    diff_lambda = 0.1 * nrm(ks[3], (DEPTH, 4, DIFF_QK_DIM), f32)
    diff_norm_g = 1.0 + 0.02 * nrm(ks[4], (DEPTH, DIFF_V_DIM), f32)
    gammas = 1.0 - jnp.exp2(-5.0 - jnp.arange(N_RET_HEADS, dtype=f32))
    base = jnp.log(-jnp.log(gammas))
    ret_log_decay = base[None, None, :] + 0.05 * nrm(ks[5], (DEPTH, 2, N_RET_HEADS), f32)
    ret_norm_g = 1.0 + 0.02 * nrm(ks[6], (DEPTH, N_RET_HEADS, RET_V_DIM), f32)
    w_out = nrm(ks[7], (DEPTH, MIX_WIDTH, D_MODEL), f32) * MIX_WIDTH ** -0.5
    ffn_norm_g = 1.0 + 0.02 * nrm(ks[8], (DEPTH, D_MODEL), f32)
    peer_w_query = nrm(ks[9], (DEPTH, D_MODEL, PEER_HEADS * PEER_KEY_DIM), f32) * D_MODEL ** -0.5
    peer_sub_keys = nrm(ks[10], (DEPTH, PEER_HEADS, 2, N_KEYS, PEER_KEY_DIM // 2), f32) * (PEER_KEY_DIM // 2) ** -0.5
    peer_u = nrm(ks[11], (DEPTH, N_EXPERTS, D_MODEL), f32) * D_MODEL ** -0.5
    peer_v = nrm(ks[12], (DEPTH, N_EXPERTS, D_MODEL), f32) * PEER_HEADS ** -0.5
    final_norm_g = 1.0 + 0.02 * nrm(ks[13], (D_MODEL,), f32)
    return {'x': x, 'attn_norm_g': attn_norm_g, 'w_in': w_in, 'diff_lambda': diff_lambda,
            'diff_norm_g': diff_norm_g, 'ret_log_decay': ret_log_decay, 'ret_norm_g': ret_norm_g,
            'w_out': w_out, 'ffn_norm_g': ffn_norm_g, 'peer_w_query': peer_w_query,
            'peer_sub_keys': peer_sub_keys, 'peer_u': peer_u, 'peer_v': peer_v,
            'final_norm_g': final_norm_g}

def first_block(x, attn_norm_g, w_in, diff_lambda, diff_norm_g, ret_log_decay, ret_norm_g,
              w_out, ffn_norm_g, peer_w_query, peer_sub_keys, peer_u, peer_v, final_norm_g):
    B, S, _ = x.shape
    pos = jnp.arange(S, dtype=jnp.float32)
    rot_dim = DIFF_QK_DIM // ROPE_FRACTION
    rope_inv = jnp.power(jnp.float32(ROPE_THETA), -jnp.arange(rot_dim // 2, dtype=jnp.float32) * 2.0 / rot_dim)
    ret_inv = 1.0 / jnp.power(jnp.float32(RET_THETA), jnp.linspace(0.0, 1.0, RET_QK_DIM // 2, dtype=jnp.float32))

    for l in range(DEPTH):
        lambda_init = 0.8 - 0.6 * math.exp(-0.3 * l)
        h = rmsnorm(x, attn_norm_g[l])
        proj = h @ w_in[l]
        dq, dk, dv, rq, rk, rv, rg = jnp.split(proj, SPLIT_POINTS, axis=-1)

        dq = rotate_prefix(dq.reshape(B, S, N_DIFF_HEADS, 2, DIFF_QK_DIM), pos, rope_inv)
        dk = rotate_prefix(dk.reshape(B, S, N_DIFF_HEADS, 2, DIFF_QK_DIM), pos, rope_inv)
        dv = dv.reshape(B, S, N_DIFF_HEADS, DIFF_V_DIM)
        lam_p = diff_lambda[l].astype(jnp.float32)
        lam = jnp.exp(jnp.sum(lam_p[0] * lam_p[1])) - jnp.exp(jnp.sum(lam_p[2] * lam_p[3])) + lambda_init
        a = diff_attention(dq, dk, dv, lam)
        a = rmsnorm(a, diff_norm_g[l]).astype(jnp.float32) * (1.0 - lambda_init)
        a = a.reshape(B, S, DIFF_WIDTH)

        rq = rotate_prefix(rq.reshape(B, S, N_RET_HEADS, RET_QK_DIM), pos, ret_inv).astype(jnp.float32)
        rk = rotate_prefix(rk.reshape(B, S, N_RET_HEADS, RET_QK_DIM), pos, ret_inv).astype(jnp.float32) * RET_QK_DIM ** -0.5
        rv = rv.reshape(B, S, N_RET_HEADS, RET_V_DIM).astype(jnp.float32)
        log_gamma = -jnp.exp(ret_log_decay[l].astype(jnp.float32))
        r_fwd = retention_direction(rq, rk, rv, log_gamma[0], False)
        r_bwd = retention_direction(rq[:, ::-1], rk[:, ::-1], rv[:, ::-1], log_gamma[1], True)[:, ::-1]
        r = group_norm(r_fwd + r_bwd, ret_norm_g[l]).reshape(B, S, RET_WIDTH)
        r = jax.nn.silu(rg.astype(jnp.float32)) * r

        mix = jnp.concatenate([a, r], axis=-1).astype(x.dtype)
        x = x + mix @ w_out[l]

        x = x + peer_ffn(rmsnorm(x, ffn_norm_g[l]), peer_w_query[l], peer_sub_keys[l], peer_u[l], peer_v[l])

    return rmsnorm(x, final_norm_g)


CONV_W = D_MODEL
CONV_K = 3
M_HEADS = 8
M_V = D_MODEL
M_DV = M_V // M_HEADS
M_DK = M_DV // 2
M_QK = M_HEADS * M_DK
QK_CONV_K = 4
CHUNK = 64
P_HEADS = 8
N_EXPERTS_2 = N_KEYS * N_KEYS
P_TOPK = 16
P_DQ = 256
P_DKH = P_DQ // 2
P_BLOCK = 128

_IN_SIZES = (CONV_W, CONV_W, CONV_W, M_QK, M_QK, M_V, M_V, M_HEADS, M_HEADS, D_MODEL, D_MODEL)
IN_WIDTH = sum(_IN_SIZES)
SPLIT_IDX = tuple(int(s) for s in np.cumsum(_IN_SIZES)[:-1])


def rms_norm(x, w):
    xf = x.astype(jnp.float32)
    y = xf * lax.rsqrt(jnp.mean(xf * xf, axis=-1, keepdims=True) + EPS)
    return (y * w.astype(jnp.float32)).astype(x.dtype)

def modulate(h, shift, scale):
    return h * (1 + scale[:, None, :]) + shift[:, None, :]

def causal_dwconv(u, w):
    K = w.shape[0]
    S = u.shape[1]
    up = jnp.pad(u, ((0, 0), (K - 1, 0), (0, 0)))
    return sum(up[:, j:j + S] * w[j] for j in range(K))

def mlstm_chunkwise(q, k, v, i_pre, f_pre):
    B, H, S, DK = q.shape
    DV = v.shape[-1]
    NC = S // CHUNK
    q = q * (DK ** -0.5)
    logf = jax.nn.log_sigmoid(f_pre)

    def chunks(t):
        return jnp.moveaxis(t.reshape(B, H, NC, CHUNK, *t.shape[3:]), 2, 0)

    xs = (chunks(q), chunks(k), chunks(v), chunks(i_pre), chunks(logf))
    mask = jnp.tril(jnp.ones((CHUNK, CHUNK), dtype=bool))

    def step(carry, inp):
        C, n, m = carry
        qb, kb, vb, ib, lfb = inp
        b = jnp.cumsum(lfb, axis=-1)
        dlog = b[..., :, None] - b[..., None, :] + ib[..., None, :]
        dlog = jnp.where(mask, dlog, -jnp.inf)
        inter = b + m[..., None]
        m_t = jnp.maximum(inter, jnp.max(dlog, axis=-1))
        w_ts = jnp.exp(dlog - m_t[..., None])
        s_qk = jnp.einsum('bhtd,bhsd->bhts', qb, kb) * w_ts
        a_inter = jnp.exp(inter - m_t)
        num = jnp.einsum('bhts,bhsv->bhtv', s_qk, vb) + a_inter[..., None] * jnp.einsum('bhtd,bhdv->bhtv', qb, C)
        den = jnp.sum(s_qk, axis=-1) + a_inter * jnp.einsum('bhtd,bhd->bht', qb, n)
        h = num / jnp.maximum(jnp.abs(den), jnp.exp(-m_t))[..., None]
        b_last = b[..., -1]
        g = b_last[..., None] - b + ib
        m_new = jnp.maximum(b_last + m, jnp.max(g, axis=-1))
        decay = jnp.exp(b_last + m - m_new)
        ws = jnp.exp(g - m_new[..., None])
        C_new = decay[..., None, None] * C + jnp.einsum('bhs,bhsd,bhsv->bhdv', ws, kb, vb)
        n_new = decay[..., None] * n + jnp.einsum('bhs,bhsd->bhd', ws, kb)
        return (C_new, n_new, m_new), h

    init = (jnp.zeros((B, H, DK, DV), jnp.float32), jnp.zeros((B, H, DK), jnp.float32), jnp.zeros((B, H), jnp.float32))
    _, hs = lax.scan(step, init, xs)
    return jnp.moveaxis(hs, 0, 2).reshape(B, H, S, DV)

def token_mixer(h, w_in, conv_a_w, conv_qk_w, b_igate, b_fgate, mh_norm_w, w_branch_a, w_branch_m, w_out):
    B, S, _ = h.shape
    proj = h @ w_in
    c_gate, b_gate, x_in, q, k, v, o, i_pre, f_pre, ga, gm = jnp.split(proj, SPLIT_IDX, axis=-1)
    ya = b_gate * causal_dwconv(c_gate * x_in, conv_a_w)
    qk = jax.nn.silu(causal_dwconv(jnp.concatenate([q, k], axis=-1), conv_qk_w))
    q, k = jnp.split(qk, 2, axis=-1)

    def to_heads(t, d):
        return t.reshape(B, S, M_HEADS, d).transpose(0, 2, 1, 3).astype(jnp.float32)

    ig = (i_pre + b_igate).transpose(0, 2, 1).astype(jnp.float32)
    fg = (f_pre + b_fgate).transpose(0, 2, 1).astype(jnp.float32)
    hm = mlstm_chunkwise(to_heads(q, M_DK), to_heads(k, M_DK), to_heads(v, M_DV), ig, fg)
    hm = hm * lax.rsqrt(jnp.mean(hm * hm, axis=-1, keepdims=True) + EPS)
    hm = hm.transpose(0, 2, 1, 3).reshape(B, S, M_V) * mh_norm_w.astype(jnp.float32)
    ym = jax.nn.sigmoid(o) * hm.astype(h.dtype)
    mix = jax.nn.sigmoid(ga) * (ya @ w_branch_a) + jax.nn.sigmoid(gm) * (ym @ w_branch_m)
    return mix @ w_out

def peer(h, wq, subkeys, u, v):
    B, S, D = h.shape
    T = B * S
    ht = h.reshape(T, D)
    q = (ht @ wq).reshape(T, P_HEADS, 2, P_DKH)
    s = jnp.einsum('thcd,hcnd->thcn', q, subkeys).astype(jnp.float32)
    s1, i1 = lax.top_k(s[:, :, 0], P_TOPK)
    s2, i2 = lax.top_k(s[:, :, 1], P_TOPK)
    cand = (s1[..., :, None] + s2[..., None, :]).reshape(T, P_HEADS, P_TOPK * P_TOPK)
    sc, ci = lax.top_k(cand, P_TOPK)
    e = jnp.take_along_axis(i1, ci // P_TOPK, axis=-1) * N_KEYS + jnp.take_along_axis(i2, ci % P_TOPK, axis=-1)
    g = jax.nn.softmax(sc, axis=-1)
    nb = T // P_BLOCK

    def block(args):
        hb, eb, gb = args
        ub = jnp.take(u, eb, axis=0)
        z = jnp.einsum('thkd,td->thk', ub, hb)
        a = (jax.nn.gelu(z.astype(jnp.float32)) * gb).astype(hb.dtype)
        return jnp.einsum('thk,thkd->td', a, jnp.take(v, eb, axis=0))

    out = lax.map(block, (ht.reshape(nb, P_BLOCK, D), e.reshape(nb, P_BLOCK, P_HEADS, P_TOPK), g.reshape(nb, P_BLOCK, P_HEADS, P_TOPK)))
    return out.reshape(B, S, D).astype(h.dtype)

def second_inputs(seed: int = 0) -> dict:
    key = jax.random.key(seed)
    ks = jax.random.split(key, 24)
    L, D = DEPTH, D_MODEL

    def nrm(k, shape, scale):
        return jax.random.normal(k, shape, jnp.float32) * scale

    return {
        "x": nrm(ks[0], (BATCH, SEQ, D), 1.0),
        "c": nrm(ks[1], (BATCH, D), 1.0),
        "w_ada": nrm(ks[2], (L, D, 6 * D), 0.2 * D ** -0.5),
        "b_ada": nrm(ks[3], (L, 6 * D), 0.02),
        "norm1_pre": 1.0 + nrm(ks[4], (L, D), 0.05),
        "norm1_post": 1.0 + nrm(ks[5], (L, D), 0.05),
        "w_in": nrm(ks[6], (L, D, IN_WIDTH), D ** -0.5),
        "conv_a_w": nrm(ks[7], (L, CONV_K, CONV_W), CONV_K ** -0.5),
        "conv_qk_w": nrm(ks[8], (L, QK_CONV_K, 2 * M_QK), QK_CONV_K ** -0.5),
        "b_igate": nrm(ks[9], (L, M_HEADS), 0.1),
        "b_fgate": jnp.linspace(3.0, 6.0, M_HEADS, dtype=jnp.float32)[None, :] + nrm(ks[10], (L, M_HEADS), 0.1),
        "mh_norm_w": 1.0 + nrm(ks[11], (L, M_V), 0.05),
        "w_branch_a": nrm(ks[12], (L, CONV_W, D), CONV_W ** -0.5),
        "w_branch_m": nrm(ks[13], (L, M_V, D), M_V ** -0.5),
        "w_out": nrm(ks[14], (L, D, D), D ** -0.5),
        "norm2_pre": 1.0 + nrm(ks[15], (L, D), 0.05),
        "norm2_post": 1.0 + nrm(ks[16], (L, D), 0.05),
        "peer_wq": nrm(ks[17], (L, D, P_HEADS * P_DQ), D ** -0.5),
        "peer_subkeys": nrm(ks[18], (L, P_HEADS, 2, N_KEYS, P_DKH), P_DKH ** -0.5),
        "peer_u": nrm(ks[19], (L, N_EXPERTS_2, D), D ** -0.5),
        "peer_v": nrm(ks[20], (L, N_EXPERTS_2, D), D ** -0.5),
    }

def second_block(x, c, w_ada, b_ada, norm1_pre, norm1_post, w_in, conv_a_w, conv_qk_w, b_igate, b_fgate, mh_norm_w, w_branch_a, w_branch_m, w_out, norm2_pre, norm2_post, peer_wq, peer_subkeys, peer_u, peer_v):
    for l in range(DEPTH):
        ada = jax.nn.silu(c) @ w_ada[l] + b_ada[l]
        sh1, sc1, g1, sh2, sc2, g2 = jnp.split(ada, 6, axis=-1)
        h = modulate(rms_norm(x, norm1_pre[l]), sh1, sc1)
        y = token_mixer(h, w_in[l], conv_a_w[l], conv_qk_w[l], b_igate[l], b_fgate[l], mh_norm_w[l], w_branch_a[l], w_branch_m[l], w_out[l])
        x = x + g1[:, None, :] * rms_norm(y, norm1_post[l])
        h = modulate(rms_norm(x, norm2_pre[l]), sh2, sc2)
        y = peer(h, peer_wq[l], peer_subkeys[l], peer_u[l], peer_v[l])
        x = x + g2[:, None, :] * rms_norm(y, norm2_post[l])
    return x


def setup_inputs(seed=0):
    out = dict(first_inputs(seed))
    for name, value in second_inputs(seed + 1).items():
        if name != "x":
            out[name + "_2"] = value
    return out


def reference(
    x, attn_norm_g, w_in, diff_lambda, diff_norm_g, ret_log_decay, ret_norm_g, w_out,
    ffn_norm_g, peer_w_query, peer_sub_keys, peer_u, peer_v, final_norm_g, c_2, w_ada_2,
    b_ada_2, norm1_pre_2, norm1_post_2, w_in_2, conv_a_w_2, conv_qk_w_2, b_igate_2, b_fgate_2,
    mh_norm_w_2, w_branch_a_2, w_branch_m_2, w_out_2, norm2_pre_2, norm2_post_2, peer_wq_2,
    peer_subkeys_2, peer_u_2, peer_v_2,
):
    x = first_block(
        x, attn_norm_g, w_in, diff_lambda, diff_norm_g, ret_log_decay, ret_norm_g, w_out,
        ffn_norm_g, peer_w_query, peer_sub_keys, peer_u, peer_v, final_norm_g,
    )
    return second_block(
        x, c_2, w_ada_2, b_ada_2, norm1_pre_2, norm1_post_2, w_in_2, conv_a_w_2, conv_qk_w_2,
        b_igate_2, b_fgate_2, mh_norm_w_2, w_branch_a_2, w_branch_m_2, w_out_2, norm2_pre_2,
        norm2_post_2, peer_wq_2, peer_subkeys_2, peer_u_2, peer_v_2,
    )


_drawn_inputs = setup_inputs


def setup_inputs(seed=0):
    import zlib

    import numpy as np

    out = dict(_drawn_inputs(seed))
    spreads = {}
    factors = {'diff_lambda': 3.338,
     'norm1_pre_2': 3.222,
     'norm1_post_2': 4.41,
     'b_igate_2': 64.0,
     'mh_norm_w_2': 6.051,
     'norm2_post_2': 8.0}
    for name, (base, spread) in spreads.items():
        noise = np.random.default_rng([zlib.crc32(name.encode()), seed]).standard_normal(out[name].shape)
        drawn = base * np.exp(spread * noise) if base else spread * noise
        out[name] = __import__('jax').numpy.asarray(drawn.astype(out[name].dtype))
    for name, factor in factors.items():
        out[name] = (out[name] * factor).astype(out[name].dtype)
    return out
```

```python
from contextlib import ExitStack

import numpy as np

import concourse.bass as bass
from concourse import mybir

F32 = mybir.dt.float32
BF16 = mybir.dt.bfloat16
U32 = mybir.dt.uint32
ALU = mybir.AluOpType
ACT = mybir.ActivationFunctionType
AX = mybir.AxisListType.X

P = 128
D = 1024
T = 512
TB = T // P
DC = D // P
EPS = 1e-6
H = 4
QK = 64
LAMBDA_INIT = 0.2
MH = 8
PH = 8
HP = 2 * PH
NK = 128
K = 16
SLOTS = PH * K
RING = 8
GROUP = 4
PAIR = 2
QUARTERS = 4
QSLOTS = SLOTS // QUARTERS
SLAB = DC * 512

N_IN1, N_OUT1, N_WQ, N_ADA, N_CONV, N_QK, N_V, N_O, N_BR, N_OUT2 = 6, 2, 4, 12, 6, 2, 2, 2, 8, 2
S_IN1 = 0
S_OUT1 = S_IN1 + N_IN1
S_WQ1 = S_OUT1 + N_OUT1
S_ADA = S_WQ1 + N_WQ
S_CONV = S_ADA + N_ADA
S_QK2 = S_CONV + N_CONV
S_V2 = S_QK2 + N_QK
S_O2 = S_V2 + N_V
S_BR = S_O2 + N_O
S_OUT2 = S_BR + N_BR
S_WQ2 = S_OUT2 + N_OUT2
N_SLABS = S_WQ2 + N_WQ


class Count:

    def __init__(self, eng, sem):
        self.eng, self.sem, self.n = eng, sem, 0

    def inc(self, ins):
        self.n = self.n + 1
        return ins.then_inc(self.sem, 1)

    def wait(self):
        self.eng.wait_ge(self.sem, self.n)


def build(nc, d, out):
    with ExitStack() as ctx:
        def sb(name, shape, dt=F32):
            return ctx.enter_context(nc.sbuf_tensor(name, shape, dt))

        def ps(name, shape):
            return ctx.enter_context(nc.psum_tensor(name, shape, F32))

        def sem(name):
            return ctx.enter_context(nc.semaphore(name))

        x_res = sb("x_res", [P, TB, D])
        xn = sb("xn", [P, TB, D])
        hT = sb("hT", [P, DC, T])
        wring = sb("wring", [P, PAIR, SLAB])
        ring = sb("ring", [P, RING * 2 * D])
        work = sb("work", [P, 8192])
        ada = sb("ada", [P, 6, D])
        ident = sb("ident_sb", [P, P])
        tri = sb("tri_sb", [P, P])
        iota = sb("iota_sb", [P, K])
        zeros = sb("zeros", [1, P + 512], BF16)
        stat = sb("stat", [P, 192])
        eid = sb("eid", [P, TB * SLOTS], U32)
        gate = sb("gate", [P, TB * SLOTS])
        idx = sb("idx", [P, 2, RING], U32)
        dots = sb("dots", [P, RING])
        gelu = sb("gelu", [P, RING])
        coef = sb("coef", [P, RING])

        proj = ps("proj", [P, 4, 512])
        tps = ps("tps", [P, 2, 512])
        obk = ps("obk", [P, 2, 512])

        rows = ring[:, :].rearrange("p (r n) -> p r n", r=RING)

        def part(t, at, n):
            return t[:, at:at + n]

        dqT = part(ring, 0, 2048).rearrange("p (c t) -> p c t", c=4)
        dkT = part(ring, 2048, 2048).rearrange("p (c t) -> p c t", c=4)
        rqkT = part(ring, 4096, 2048).rearrange("p (c t) -> p c t", c=4)
        dv = part(ring, 6144, 2048).rearrange("p (b n) -> p b n", b=TB)
        rv = part(ring, 8192, 2048).rearrange("p (b n) -> p b n", b=TB)
        rg = part(ring, 10240, 2048).rearrange("p (b n) -> p b n", b=TB)
        NTOE = 2 * T - P
        decay = part(ring, 12288, H * NTOE).rearrange("p (h n) -> p h n", h=H)
        rope = part(ring, 15872, 320)
        cosd = part(rope, 0, 32).rearrange("p (b n) -> p b n", b=TB)
        sind = part(rope, 32, 32).rearrange("p (b n) -> p b n", b=TB)
        cosr = part(rope, 64, 128).rearrange("p (b n) -> p b n", b=TB)
        sinr = part(rope, 192, 128).rearrange("p (b n) -> p b n", b=TB)
        stg = xn[:, :, :].rearrange("p b n -> p (b n)").rearrange("p (s b n) -> p s b n", s=2, b=TB)
        gain1 = part(work, 0, D)
        gain2 = ada[:, 2, :]
        rtmp = part(work, 1024, 4096).rearrange("p (k n) -> p k n", k=4)
        dist = part(work, 5120, 2 * NTOE).rearrange("p (k n) -> p k n", k=2)
        diffg = ada[:, 0, 0:P]
        retg = ada[:, 0, P:P + H * P]
        lamp = ada[:, 1, 0:4 * QK]
        rdec = ada[:, 1, 256:264]
        prob = part(work, 0, 2048).rearrange("p (k m n) -> p k m n", k=2, m=2)
        atile = part(work, 2048, 1024).rearrange("p (k n) -> p k n", k=2)
        aT = part(work, 3072, 1024).rearrange("p (k n) -> p k n", k=2)
        rP = part(work, 4096, 4096).rearrange("p (k j n) -> p k j n", k=2, j=TB)
        sq16 = part(work, 0, 2048).rearrange("p (b h n) -> p b h n", b=TB, h=H)

        subk = part(ring, 0, HP * NK).rearrange("p (g n) -> p g n", g=HP)
        qT = part(ring, 2048, 2048).rearrange("p (k t) -> p k t", k=4)
        srep = part(ring, 4096, 1024).rearrange("p (k b n) -> p k b n", k=2, b=TB)
        topu = part(ring, 5120, 1024).bitcast(U32).rearrange("p (b g k) -> p b g k", b=TB, g=HP)
        tops = part(work, 0, 1024).rearrange("p (b g k) -> p b g k", b=TB, g=HP)
        topi = part(work, 1024, 1024).rearrange("p (b g k) -> p b g k", b=TB, g=HP)
        small = part(work, 2048, 1024)
        loc_s = part(small, 0, 256).rearrange("p (h c k) -> p h c k", h=PH, c=2)
        loc_i = part(small, 256, 256).rearrange("p (h c k) -> p h c k", h=PH, c=2)
        best = part(small, 512, 128).rearrange("p (h k) -> p h k", h=PH)
        posu = part(small, 640, 128).bitcast(U32).rearrange("p (h k) -> p h k", h=PH)
        half_u = part(small, 768, 128).bitcast(U32).rearrange("p (h k) -> p h k", h=PH)
        half_f = part(small, 896, 128).rearrange("p (h k) -> p h k", h=PH)
        idf = part(work, 3072, 256).rearrange("p (c h k) -> p c h k", c=2, h=PH)
        expg = part(work, 3328, 128).rearrange("p (h k) -> p h k", h=PH)
        eidf = part(work, 3456, 128).rearrange("p (h k) -> p h k", h=PH)
        hflat = hT[:, :, :].rearrange("p c t -> p (c t)")
        cand = part(hflat, 0, 2048).rearrange("p (h i j) -> p h i j", h=PH, i=K)
        cand2 = part(hflat, 2048, 2048).rearrange("p (h n) -> p h n", h=PH)
        onehot = part(hflat, 2048, 2048).rearrange("p (h k j) -> p h k j", h=PH, k=K)
        late = part(work, 3584, 2 * D).rearrange("p (k n) -> p k n", k=2)
        cbc = part(work, 6144, 1024).rearrange("p (c m) -> p c m", c=DC)
        diag = part(work, 7168, 1024).rearrange("p (r m) -> p r m", r=RING)

        vaug = part(ring, 0, TB * MH * (P + 1)).rearrange("p (b h n) -> p b h n", b=TB, h=MH)
        yaT = part(ring, 4128, 4096).rearrange("p (c t) -> p c t", c=DC)
        qT2 = part(ring, 8224, 2048).rearrange("p (c t) -> p c t", c=4)
        kT2 = part(ring, 10272, 2048).rearrange("p (c t) -> p c t", c=4)
        mixT = part(ring, 8224, 4096).rearrange("p (c t) -> p c t", c=DC)
        ymT = part(ring, 0, 4096).rearrange("p (c t) -> p c t", c=DC)
        NPT = sum(T - P * s for s in range(TB))
        mP = part(ring, 12320, 2 * NPT).rearrange("p (k n) -> p k n", k=2)
        wts = part(ring, 12320 + 2 * NPT, 1024).rearrange("p (k n) -> p k n", k=2)
        convw = part(ring, 16384 - 64, 56)
        hm = part(work, 0, 4096).rearrange("p (b h n) -> p b h n", b=TB, h=MH)
        hmw = part(work, 0, 4096).rearrange("p (b n) -> p b n", b=TB)
        mrow = part(work, 4096, 2560).rearrange("p (k t) -> p k t", k=5)
        sel = part(work, 6656, MH * P).rearrange("p (h m) -> p h m", h=MH)
        cx = part(work, 0, 2 * 516).rearrange("p (k n) -> p k n", k=2)
        csb = part(work, 1040, 1024).rearrange("p (k n) -> p k n", k=2)
        ctmp = part(work, 2064, 1024).rearrange("p (k n) -> p k n", k=2)
        sig = part(work, 5120, 2048).rearrange("p (k n) -> p k n", k=4)
        br1 = part(work, 7168, 1024).rearrange("p (k n) -> p k n", k=2)
        mhg = part(work, 4096, D)
        post = part(work, 4096, 3 * D).rearrange("p (k n) -> p k n", k=3)
        wif = part(work, 7680, 128).rearrange("p (c n) -> p c n", c=DC)
        bif = stat[0:MH, 188:190]
        acol = part(stat, 100, 32).rearrange("p (b h) -> p b h", b=TB)
        ecol = part(stat, 132, 32).rearrange("p (b h) -> p b h", b=TB)
        ss = part(stat, 0, 4)
        rstd = part(stat, 4, 4)
        mx = part(stat, 8, 4).rearrange("p (k m) -> p k m", k=2)
        nmx = part(stat, 12, 4).rearrange("p (k m) -> p k m", k=2)
        psum = part(stat, 16, 4).rearrange("p (k m) -> p k m", k=2)
        pinv = part(stat, 20, 4).rearrange("p (k m) -> p k m", k=2)
        lam = part(stat, 24, 4)
        lgam = part(stat, 28, 8)
        st16 = part(stat, 36, 16).rearrange("p (b h) -> p b h", b=TB)
        sv16 = part(stat, 52, 16).rearrange("p (b h) -> p b h", b=TB)
        st32 = part(stat, 36, 32).rearrange("p (b h) -> p b h", b=TB)
        dinv = part(stat, 68, 4)
        den = part(stat, 72, 4)
        silc = part(stat, 76, 8)
        epsc = part(stat, 164, 1)
        ccol = part(stat, 84, 8)
        gsum = part(stat, 92, 8)

        in_x, in_cst, in_g1, in_blk1 = sem("in_x"), sem("in_cst"), sem("in_g1"), sem("in_blk1")
        in_keys, in_bias, in_late, in_conv = sem("in_keys"), sem("in_bias"), sem("in_late"), sem("in_conv")
        in_lstm, in_mhg, in_post, stored = sem("in_lstm"), sem("in_mhg"), sem("in_post"), sem("stored")
        slab = [sem(f"slab{k}") for k in range(PAIR)]
        row = [sem(f"row{r}") for r in range(RING)]
        mm_done, mm_free = sem("mm_done"), sem("mm_free")
        tr_done, tr_free = sem("tr_done"), sem("tr_free")
        rms_done, xn_ready, x_ready = sem("rms_done"), sem("xn_ready"), sem("x_ready")
        rotated, lam_arg, lam_exp = sem("rotated"), sem("lam_arg"), sem("lam_exp")
        dec_arg, dec_done = sem("dec_arg"), sem("dec_done")
        sc_done, sc_max, sc_exp, a_ready = sem("sc_done"), sem("sc_max"), sem("sc_exp"), sem("a_ready")
        o_done, o_free, hn_arg, hn_done = sem("o_done"), sem("o_free"), sem("hn_arg"), sem("hn_done")
        rs_done, rp_ready, mix_ready = sem("rs_done"), sem("rp_ready"), sem("mix_ready")
        key_done, key_free = sem("key_done"), sem("key_free")
        g_arg, g_exp, eid_ready, idx_ready = sem("g_arg"), sem("g_exp"), sem("eid_ready"), sem("idx_ready")
        dot_done, gelu_done, coef_done, diag_ready = sem("dot_done"), sem("gelu_done"), sem("coef_done"), sem("diag_ready")
        slot_free, acc_done, acc_free = sem("slot_free"), sem("acc_done"), sem("acc_free")
        zeros_set, out_ready, paced = sem("zeros_set"), sem("out_ready"), sem("paced")
        c_silu, cbc_ready, c_copied, qk_conv, qk_ready = (sem("c_silu"), sem("cbc_ready"), sem("c_copied"),
                                                          sem("qk_conv"), sem("qk_ready"))
        v_ones, if_done, if_act, ln_done = sem("v_ones"), sem("if_done"), sem("if_act"), sem("ln_done")
        rows_ready, cols_done, cols_ready, nm_done = sem("rows_ready"), sem("cols_done"), sem("cols_ready"), sem("nm_done")
        w_arg, w_exp, p_ready, num_done, num_free = (sem("w_arg"), sem("w_exp"), sem("p_ready"), sem("num_done"),
                                                     sem("num_free"))
        ym_part, g_sig, mixT_ready = sem("ym_part"), sem("g_sig"), sem("mixT_ready")
        vec, act_s = sem("vec"), sem("act_s")

        block = ctx.enter_context(nc.Block())

        TR_N1 = 0
        TR_QK = TR_N1 + 8
        TR_A = TR_QK + 12
        TR_MIX = TR_A + 16
        TR_F1 = TR_MIX + 8
        TR_N2 = TR_F1 + 8
        TR_YM = TR_N2 + 8
        TR_F2 = TR_YM + 8

        @block.sync
        def _(sp):
            sp.dma_start(x_res[:, :, :], d["x"].rearrange("(b p) n -> p b n", p=P)).then_inc(in_x, 16)
            for k in range(PAIR):
                sp.dma_start(wring[:, k, :], d["slabs"][k]).then_inc(slab[k], 16)
            with sp.Fori(1, N_SLABS // PAIR) as pair:
                for k in range(PAIR):
                    sp.wait_ge(mm_done, pair * (4 * PAIR) + (4 * k - 4))
                    sp.dma_start(wring[:, k, :], d["slabs"][bass.ds(pair * PAIR + k, 1)].rearrange("s p n -> (s p) n")).then_inc(slab[k], 16)
            with sp.Fori(0, TB) as tb:
                sp.wait_ge(out_ready, tb + 1)
                sp.dma_start(out[bass.ts(tb, P), :], x_res[:, bass.ds(tb, 1), :].rearrange("p b n -> p (b n)")).then_inc(stored, 16)
            sp.wait_ge(stored, 16 * TB)

        @block.gpsimd
        def _(pool):
            def gather(layer):
                with pool.Fori(0, TB) as tb:
                    pool.wait_ge(eid_ready, tb + (layer * TB + 1))
                    pool.sem_inc(paced, 1)
                    with pool.Fori(0, SLOTS // (2 * RING)) as it:
                        for k in range(2):
                            slot = tb * SLOTS + it * (2 * RING) + k * RING
                            pool.tensor_copy(idx[:, k, :], eid[:, bass.ds(slot, RING)]).then_inc(idx_ready, 1)
                            first = tb * (SLOTS // RING) + it * 2 + (layer * TB * SLOTS // RING + k + 1)
                            pool.wait_ge(idx_ready, first)
                            for r in range(RING):
                                pool.wait_ge(slot_free, slot + (layer * TB * SLOTS + r + 1))
                                pool.sem_inc(paced, 1)
                                pool.indirect_dma_start(
                                    rows[:, r, :], None, d[f"experts{layer + 1}"],
                                    bass.IndirectOffsetOnAxis(idx[:, k, r:r + 1], 0)).then_inc(row[r], 16)

            gather(0)
            gather(1)

        @block.tensor
        def _(pe):
            def transposes(job, sources):
                if job >= 2:
                    pe.wait_ge(tr_free, job - 1)
                for k, s in enumerate(sources):
                    t = pe.transpose(tps[:, job % 2, k * P:(k + 1) * P], s, ident[:, :])
                t.then_inc(tr_done, 1)

            def norm_transposes(job, src, ready, count, per):
                for tb in range(TB):
                    pe.wait_ge(ready, count + per * (tb + 1))
                    for k in range(2):
                        transposes(job + 2 * tb + k, [src[:, tb, (4 * k + c) * P:(4 * k + c + 1) * P] for c in range(4)])

            def slab_landed(k, pair):
                pe.wait_ge(slab[k], pair * 16 + 16)

            def bank_free(job):
                pe.wait_ge(mm_free, job + 1)

            def token_major(first, n, lhs):
                with pe.Fori(0, n // PAIR) as it:
                    pair = it + first // PAIR
                    for k in range(PAIR):
                        slab_landed(k, pair)
                        for tb in range(TB):
                            bank_free(pair * 8 + (4 * k + tb))
                            for c in range(DC):
                                m = pe.matmul(proj[:, tb, :], lhs[:, c, tb * P:(tb + 1) * P],
                                              wring[:, k, c * 512:(c + 1) * 512], start=(c == 0), stop=(c == DC - 1))
                            m.then_inc(mm_done, 1)

            def transposed_tile(k, j, rhs):
                for c in range(DC):
                    at = (j * DC + c) * P
                    m = pe.matmul(proj[:, j, :], wring[:, k, at:at + P], rhs[:, c, :],
                                  start=(c == 0), stop=(c == DC - 1))
                m.then_inc(mm_done, 1)

            def all_read(first):
                pe.wait_ge(mm_free, 4 * first + 4)

            def transposed(first, n, rhs):
                with pe.Fori(0, n // PAIR) as it:
                    pair = it + first // PAIR
                    for k in range(PAIR):
                        slab_landed(k, pair)
                        for j in range(4):
                            bank_free(pair * 8 + (4 * k + j))
                            transposed_tile(k, j, rhs)

            pe.wait_ge(in_cst, 32)
            norm_transposes(TR_N1, xn, xn_ready, 0, 1)
            pe.wait_ge(tr_free, TR_N1 + 8)

            def turn_staged(n, src):
                pe.wait_ge(rotated, n + 1)
                for tb in range(TB):
                    transposes(TR_QK + 4 * n + tb, [stg[:, src, tb, c * P:(c + 1) * P] for c in range(4)])

            pe.wait_ge(zeros_set, 1)
            token_major(S_IN1, 4, hT)
            turn_staged(0, 0)
            turn_staged(1, 1)
            token_major(S_IN1 + 4, 2, hT)
            turn_staged(2, 0)

            units = [(h, tb) for h in range(H) for tb in range(TB)]
            pe.wait_ge(tr_free, TR_QK + 12)
            all_read(S_OUT1)

            def scores(n):
                h, tb = units[n]
                if n >= 2:
                    pe.wait_ge(sc_exp, n - 1)
                for m in range(2):
                    q = slice(QK * m, QK * m + QK)
                    s = pe.matmul(proj[:, 2 * (n % 2) + m, :], dqT[q, h, tb * P:(tb + 1) * P], dkT[q, h, :],
                                  start=True, stop=True)
                s.then_inc(sc_done, 1)

            def turn(n):
                pe.wait_ge(a_ready, n + 1)
                transposes(TR_A + n, [atile[:, n % 2, c * P:(c + 1) * P] for c in range(4)])

            def weigh(n):
                h, tb = units[n]
                pe.wait_ge(tr_free, TR_A + n + 1)
                if n >= 2:
                    pe.wait_ge(o_free, n - 1)
                for c in range(TB):
                    o = pe.matmul(obk[:, n % 2, 0:P], aT[:, n % 2, c * P:(c + 1) * P], dv[:, c, h * P:(h + 1) * P],
                                  start=(c == 0), stop=(c == TB - 1))
                o.then_inc(o_done, 1)

            scores(0)
            for n in range(1, len(units) + 2):
                if n < len(units):
                    scores(n)
                if n >= 2:
                    turn(n - 2)
                if n >= 3:
                    weigh(n - 3)
            weigh(len(units) - 1)

            pe.wait_ge(sc_exp, len(units))

            def ret_scores(h):
                q = slice(QK * (h % 2), QK * (h % 2) + QK)
                for j in range(TB):
                    if h:
                        pe.wait_ge(rp_ready, TB * (h - 1) + j + 1)
                    pe.matmul(proj[:, j, :], rqkT[q, 2 + h // 2, j * P:(j + 1) * P], rqkT[q, h // 2, :],
                              start=True, stop=True).then_inc(rs_done, 1)

            def ret_values(h):
                n = len(units) + h
                pe.wait_ge(rp_ready, TB * (h + 1))
                pe.wait_ge(o_free, n - 1)
                for i in range(TB):
                    for j in range(TB):
                        o = pe.matmul(obk[:, n % 2, i * P:(i + 1) * P], rP[:, h % 2, j, i * P:(i + 1) * P],
                                      rv[:, j, h * P:(h + 1) * P], start=(j == 0), stop=(j == TB - 1))
                o.then_inc(o_done, 1)

            for h in range(H + 1):
                if h < H:
                    ret_scores(h)
                if h:
                    ret_values(h - 1)
            norm_transposes(TR_MIX, xn, mix_ready, 1, 0)
            pe.wait_ge(tr_free, TR_MIX + 8)
            token_major(S_OUT1, N_OUT1, hT)

            def route(layer, first):
                all_read(first)
                pe.wait_ge(in_keys, 16 * (layer + 1))
                with pe.Fori(0, N_WQ // PAIR) as it:
                    pair = it + first // PAIR

                    def key_scores(g):
                        pe.wait_ge(mm_free, pair * 8 + (g + 1 + 4))
                        pe.wait_ge(key_free, it * 8 + (layer * HP + g + 1))
                        bank = tps if g % 4 < 2 else obk
                        for tb in range(TB):
                            s = pe.matmul(bank[:, g % 2, tb * P:(tb + 1) * P], qT[:, g % 4, tb * P:(tb + 1) * P],
                                          keys(it, g), start=True, stop=True)
                        s.then_inc(key_done, 1)

                    for g in range(8):
                        if g % 4 == 0:
                            slab_landed(g // 4, pair)
                        bank_free(pair * 8 + g)
                        transposed_tile(g // 4, g % 4, hT)
                        if g:
                            key_scores(g - 1)
                    key_scores(7)
                pe.wait_ge(key_free, layer * HP + HP + 4)

            def keys(it, g):
                return subk[:, bass.ds(it * 8 + g, 1), :].rearrange("p g n -> p (g n)")

            def clear_sum(start):
                for c in range(2):
                    z = pe.matmul(obk[:, c, :], zeros[0:1, 0:P], zeros[0:1, P:P + 512], start=start,
                                  stop=not start, skip_group_check=True)
                return z

            def weigh_experts(slot, n):
                with pe.Fori(0, n // RING) as it:
                    for r in range(RING):
                        pe.wait_ge(diag_ready, it * RING + slot + (r + 1))
                        for c in range(2):
                            m = pe.matmul(obk[:, c, :], diag[:, r, :], rows[:, r, D + c * 512:D + (c + 1) * 512],
                                          start=False, stop=False, skip_group_check=True)
                        m.then_inc(slot_free, 1)

            norm_transposes(TR_F1, xn, xn_ready, TB, 1)
            pe.wait_ge(tr_free, TR_F1 + 8)
            route(0, S_WQ1)
            pe.wait_ge(cbc_ready, 1)
            all_read(S_ADA)

            def modulation(n):
                k = (S_ADA + n) % PAIR
                pe.wait_ge(slab[k], 16 * ((S_ADA + n) // PAIR + 1))
                if n >= 4:
                    pe.wait_ge(mm_free, 4 * (S_ADA + n - 3) + 4)
                for c in range(DC):
                    m = pe.matmul(proj[:, n % 4, :], cbc[:, c, :], wring[:, k, c * 512:(c + 1) * 512],
                                  start=(c == 0), stop=(c == DC - 1))
                m.then_inc(mm_done, 4)

            for tb in range(TB):
                pe.wait_ge(acc_free, tb + 1)
                clear_sum(True)
                for q in range(QUARTERS):
                    if q < N_ADA // TB:
                        modulation(tb * (N_ADA // TB) + q)
                    weigh_experts(tb * SLOTS + q * QSLOTS, QSLOTS)
                clear_sum(False).then_inc(acc_done, 1)

            norm_transposes(TR_N2, xn, xn_ready, 2 * TB, 1)
            pe.wait_ge(tr_free, TR_N2 + 8)
            all_read(S_CONV)
            transposed(S_CONV, N_CONV, hT)
            all_read(S_QK2)
            transposed(S_QK2, N_QK, hT)
            all_read(S_V2)
            token_major(S_V2, N_V, hT)
            pe.wait_ge(in_lstm, 16 * 4)
            for g in range(2):
                for c in range(DC):
                    m = pe.matmul(obk[0:MH, g, :], wif[:, c, g * MH:(g + 1) * MH], hT[:, c, :],
                                  start=(c == 0), stop=(c == DC - 1))
            m.then_inc(if_done, 1)

            pe.wait_ge(rows_ready, 1)
            for g, r in enumerate((2, 4)):
                for b in range(TB):
                    t = pe.transpose(tps[:, g, b * MH:(b + 1) * MH], mrow[0:MH, r, b * P:(b + 1) * P], ident[0:MH, 0:MH])
            t.then_inc(cols_done, 1)
            pe.wait_ge(cols_ready, 2)
            all_read(S_O2)
            pe.wait_ge(qk_ready, 8)
            pe.wait_ge(v_ones, 1)

            def gate_rows(h):
                if h >= 2:
                    pe.wait_ge(w_arg, TB * (h - 1))
                pe.matmul(tps[:, h % 2, :], sel[0:MH, h, :], mrow[0:MH, 3, :], start=True, stop=True).then_inc(nm_done, 1)

            def lstm_scores(h):
                q = slice(QK * (h % 2), QK * (h % 2) + QK)
                for s in range(TB):
                    if h:
                        pe.wait_ge(p_ready, TB * (h - 1) + s + 1)
                    pe.matmul(proj[:, s, s * P:T], kT2[q, h // 2, s * P:(s + 1) * P], qT2[q, h // 2, s * P:T],
                              start=True, stop=True).then_inc(rs_done, 1)

            def lstm_values(h):
                pe.wait_ge(p_ready, TB * (h + 1))
                if h:
                    pe.wait_ge(num_free, h)
                for b in range(TB):
                    for s in range(b + 1):
                        at = sum(T - P * u for u in range(s)) + (b - s) * P
                        m = pe.matmul(obk[:, b // 2, (b % 2) * 256:(b % 2) * 256 + P + 1], mP[:, h % 2, at:at + P],
                                      vaug[:, s, h, :], start=(s == 0), stop=(s == b))
                m.then_inc(num_done, 1)

            for h in range(MH + 1):
                if h < MH:
                    gate_rows(h)
                    lstm_scores(h)
                if h:
                    lstm_values(h - 1)
            pe.wait_ge(num_free, MH)
            token_major(S_O2, N_O, hT)
            pe.wait_ge(ym_part, N_O * TB)
            for tb in range(TB):
                for k in range(2):
                    transposes(TR_YM + 2 * tb + k, [hmw[:, tb, (4 * k + c) * P:(4 * k + c + 1) * P] for c in range(4)])
            pe.wait_ge(tr_free, TR_YM + 8)
            all_read(S_BR)
            with pe.Fori(0, N_BR // PAIR) as it:
                pair = it + S_BR // PAIR
                for k in range(PAIR):
                    slab_landed(k, pair)
                    for j, rhs in enumerate((hT, yaT, hT, ymT)):
                        bank_free(pair * 8 + (4 * k + j))
                        transposed_tile(k, j, rhs)
            all_read(S_OUT2)
            pe.wait_ge(mixT_ready, DC)
            token_major(S_OUT2, N_OUT2, mixT)
            norm_transposes(TR_F2, xn, xn_ready, 3 * TB, 1)
            pe.wait_ge(tr_free, TR_F2 + 8)
            route(1, S_WQ2)
            with pe.Fori(0, TB) as tb:
                pe.wait_ge(acc_free, tb + (TB + 1))
                clear_sum(True)
                weigh_experts(tb * SLOTS + TB * SLOTS, SLOTS)
                clear_sum(False).then_inc(acc_done, 1)

        @block.scalar
        def _(act):
            steps = Count(act, act_s)
            for t, n in ((gain1, "attn_norm_g"),):
                act.dma_start(t, d[n]).then_inc(in_g1, 16)
            for t, n in ((ident[:, :], "ident"), (iota[:, :], "iota")):
                act.dma_start(t, d[n]).then_inc(in_cst, 16)
            for t, n in ((rope, "rope"), (part(work, 5120, 2 * NTOE), "dist"), (diffg, "diff_norm_g"),
                         (retg, "ret_norm_g"), (lamp, "diff_lambda"), (rdec, "ret_log_decay"), (ccol, "c_2"),
                         (gain2, "ffn_norm_g")):
                act.dma_start(t, d[n]).then_inc(in_blk1, 16)

            def root(dst, src, n, done):
                act.activation(dst, src, ACT.Sqrt, bias=epsc, scale=1.0 / n).then_inc(done, 1)

            def rms(src, ready):
                for tb in range(TB):
                    ready(tb)
                    steps.inc(act.activation(xn[:, tb, :], src[:, tb, :], ACT.Square, accum_out=ss[:, tb:tb + 1]))
                steps.wait()
                root(rstd, ss, D, rms_done)

            def turned(job, n, dst):
                for j in range(n):
                    act.wait_ge(tr_done, job + j + 1)
                    act.activation(dst(j), tps[:, (job + j) % 2, :].rearrange("p (c t) -> p c t", c=4),
                                   ACT.Copy).then_inc(tr_free, 1)

            def norm_turned(job, t):
                turned(job, 2 * TB, lambda j: t[:, 4 * (j % 2):4 * (j % 2) + 4, (j // 2) * P:(j // 2 + 1) * P])

            def take(s, tb, dst, func):
                act.wait_ge(mm_done, 4 * s + tb + 1)
                act.activation(dst, proj[:, tb, :], func).then_inc(mm_free, 1)

            act.wait_ge(zeros_set, 1)
            rms(x_res, lambda tb: act.wait_ge(in_x, 16))
            norm_turned(TR_N1, hT)

            for tb in range(TB):
                take(0, tb, stg[:, 0, tb, :], ACT.Copy)
            for tb in range(TB):
                take(1, tb, stg[:, 1, tb, :], ACT.Copy)
            for tb in range(TB):
                take(2, tb, dv[:, tb, :], ACT.Copy)
            turned(TR_QK, 4, lambda j: dqT[:, :, j * P:(j + 1) * P])
            for tb in range(TB):
                take(3, tb, stg[:, 0, tb, :], ACT.Copy)
            turned(TR_QK + 4, 4, lambda j: dkT[:, :, j * P:(j + 1) * P])
            for tb in range(TB):
                take(4, tb, rv[:, tb, :], ACT.Copy)
            for tb in range(TB):
                take(5, tb, rg[:, tb, :], ACT.Silu)
            turned(TR_QK + 8, 4, lambda j: rqkT[:, :, j * P:(j + 1) * P])

            act.wait_ge(lam_arg, 1)
            act.activation(lam[:, 2:4], lam[:, 0:2], ACT.Exp).then_inc(lam_exp, 1)
            act.activation(lgam, rdec, ACT.Exp).then_inc(lam_exp, 1)
            for h in range(H):
                act.wait_ge(dec_arg, h + 1)
                act.activation(decay[:, h, :], decay[:, h, :], ACT.Exp).then_inc(dec_done, 1)

            def exps(n):
                act.wait_ge(sc_max, n + 1)
                if n >= 2:
                    act.wait_ge(a_ready, n - 1)
                for m in range(2):
                    e = act.activation(prob[:, n % 2, m, :], proj[:, 2 * (n % 2) + m, :], ACT.Exp,
                                       bias=nmx[:, n % 2, m:m + 1], scale=QK ** -0.5, accum_out=psum[:, n % 2, m:m + 1])
                e.then_inc(sc_exp, 1)

            def a_turned(n):
                act.wait_ge(tr_done, TR_A + n + 1)
                if n >= 2:
                    act.wait_ge(o_done, n - 1)
                act.activation(aT[:, n % 2, :], tps[:, (TR_A + n) % 2, :], ACT.Copy).then_inc(tr_free, 1)

            def o_taken(n):
                h, tb = divmod(n, TB)
                act.wait_ge(o_done, n + 1)
                act.activation(xn[:, tb, h * P:(h + 1) * P], obk[:, n % 2, 0:P], ACT.Copy).then_inc(o_free, 1)

            for n in range(H * TB + 3):
                if n < H * TB:
                    exps(n)
                if 2 <= n < H * TB + 2:
                    a_turned(n - 2)
                if n >= 3:
                    o_taken(n - 3)
            for h in range(H):
                n = H * TB + h
                act.wait_ge(o_done, n + 1)
                act.activation(xn[:, :, 512 + h * P:512 + (h + 1) * P],
                               obk[:, n % 2, :].rearrange("p (b n) -> p b n", b=TB), ACT.Copy).then_inc(o_free, 1)
            act.wait_ge(hn_arg, 1)
            root(st16, st16, P, hn_done)
            act.wait_ge(hn_arg, 2)
            root(sv16, sv16, P, hn_done)
            norm_turned(TR_MIX, hT)
            act.activation(silc, ccol, ACT.Silu).then_inc(c_silu, 1)

            def route(layer, first):
                with act.Fori(0, N_WQ // PAIR) as it:
                    for g in range(8):
                        act.wait_ge(mm_done, it * 8 + (4 * first + g + 1))
                        act.wait_ge(key_done, it * 8 + (layer * HP + g + 1))
                        act.activation(qT[:, g % 4, :], proj[:, g % 4, :], ACT.Copy).then_inc(mm_free, 1)

            def gates(layer, tb):
                act.wait_ge(g_arg, layer * TB + tb + 1)
                act.activation(expg, expg, ACT.Exp).then_inc(g_exp, 1)

            def gelus(layer, tb, q, func):
                with act.Fori(0, QSLOTS // RING) as it:
                    for g in range(RING // GROUP):
                        act.wait_ge(dot_done, it * RING + ((layer * TB + tb) * SLOTS + q * QSLOTS + (g + 1) * GROUP))
                        act.activation(gelu[:, g * GROUP:(g + 1) * GROUP], dots[:, g * GROUP:(g + 1) * GROUP],
                                       func).then_inc(gelu_done, 1)

            rms(x_res, lambda tb: act.wait_ge(mm_free, 4 * (S_OUT1 + 1) + tb + 1 + 4))
            norm_turned(TR_F1, hT)
            act.dma_start(subk, d["keys1"]).then_inc(in_keys, 16)
            act.dma_start(ada[:, :, :], d["b_ada_2"]).then_inc(in_bias, 16)
            act.dma_start(late[:, 0, :], d["final_norm_g"]).then_inc(in_late, 16)
            act.dma_start(late[:, 1, :], d["norm1_pre_2"]).then_inc(in_late, 16)
            route(0, S_WQ1)
            gates(0, 0)
            for tb in range(TB):
                for q in range(QUARTERS):
                    gelus(0, tb, q, ACT.Gelu)
                    if q == 0 and tb + 1 < TB:
                        gates(0, tb + 1)

            rms(x_res, lambda tb: act.wait_ge(acc_free, tb + 2))
            rms(x_res, lambda tb: act.wait_ge(x_ready, tb + 1))
            act.dma_start(convw, d["conv_w"]).then_inc(in_conv, 16)
            for t, n in ((tri[:, :], "tri"), (bif, "b_if"), (wif, "w_if"), (sel[0:MH, :, :], "sel")):
                act.dma_start(t, d[n]).then_inc(in_lstm, 16)
            norm_turned(TR_N2, hT)
            for j in range(DC):
                job = 4 * S_CONV + 3 * j
                act.wait_ge(mm_done, job + 1)
                if j >= 2:
                    act.wait_ge(mm_free, job - 3 + 4)
                act.activation(csb[:, j % 2, :], proj[:, job % 4, :], ACT.Copy).then_inc(c_copied, 1)
            act.wait_ge(mm_free, 4 * S_QK2 + 4)
            act.wait_ge(qk_conv, 1)

            def qk_silu(j):
                act.wait_ge(qk_conv, j + 2)
                act.activation((qT2 if j < 4 else kT2)[:, j % 4, :], ctmp[:, j % 2, :], ACT.Silu).then_inc(qk_ready, 1)

            for j in range(N_QK * 4):
                act.wait_ge(mm_done, 4 * S_QK2 + j + 1)
                if j >= 2:
                    act.wait_ge(qk_conv, j)
                act.activation(cx[:, j % 2, 3:3 + T], proj[:, j % 4, :], ACT.Copy).then_inc(mm_free, 1)
                if j:
                    qk_silu(j - 1)
            qk_silu(N_QK * 4 - 1)
            for s in range(N_V):
                for tb in range(TB):
                    act.wait_ge(mm_done, 4 * (S_V2 + s) + tb + 1)
                    act.activation(vaug[:, tb, 4 * s:4 * s + 4, 0:P], proj[:, tb, :].rearrange("p (h n) -> p h n", h=4),
                                   ACT.Copy).then_inc(mm_free, 1)

            act.wait_ge(if_act, 1)
            steps.inc(act.activation(mrow[0:MH, 0, :], mrow[0:MH, 1, :], ACT.Abs))
            steps.wait()
            steps.inc(act.activation(mrow[0:MH, 0, :], mrow[0:MH, 0, :], ACT.Exp, scale=-1.0))
            steps.wait()
            act.activation(mrow[0:MH, 0, :], mrow[0:MH, 0, :], ACT.Ln, bias=1.0).then_inc(ln_done, 1)
            act.wait_ge(if_act, 2)
            act.activation(mrow[0:MH, 4, :], mrow[0:MH, 4, :], ACT.Exp, scale=-1.0).then_inc(rows_ready, 1)
            act.dma_start(mhg, d["mh_norm_w_2"]).then_inc(in_mhg, 16)
            act.wait_ge(cols_done, 1)
            for g, t in enumerate((acol, ecol)):
                act.activation(t, tps[:, g, 0:TB * MH].rearrange("p (b h) -> p b h", b=TB),
                               ACT.Copy).then_inc(cols_ready, 1)
            for n in range(MH * TB):
                s = n % TB
                act.wait_ge(w_arg, n + 1)
                act.activation(wts[:, n % 2, s * P:T], wts[:, n % 2, s * P:T], ACT.Exp).then_inc(w_exp, 1)
            act.wait_ge(hn_arg, 3)
            root(st32, st32, P, hn_done)
            for n in range(N_O * TB):
                act.wait_ge(mm_done, 4 * S_O2 + n + 1)
                if n >= 4:
                    act.wait_ge(ym_part, n - 3)
                act.activation(sig[:, n % 4, :], proj[:, n % 4, :], ACT.Sigmoid).then_inc(mm_free, 1)
            norm_turned(TR_YM, ymT)
            for n in range(2 * DC):
                act.wait_ge(mm_done, 4 * S_BR + 2 * n + 1)
                if n >= 4:
                    act.wait_ge(mixT_ready, (n - 4) // 2 + 1)
                act.activation(sig[:, n % 4, :], proj[:, (2 * n) % 4, :], ACT.Sigmoid).then_inc(g_sig, 1)
            act.wait_ge(mixT_ready, DC)
            for k, n in enumerate(("norm1_post_2", "norm2_pre_2", "norm2_post_2")):
                act.dma_start(post[:, k, :], d[n]).then_inc(in_post, 16)
            act.dma_start(subk, d["keys2"]).then_inc(in_keys, 16)
            for s in range(N_OUT2):
                for tb in range(TB):
                    take(S_OUT2 + s, tb, hmw[:, tb, s * 512:(s + 1) * 512], ACT.Copy)
            act.wait_ge(mm_free, 4 * S_WQ2 + 4)
            rms(hmw, lambda tb: None)
            rms(x_res, lambda tb: act.wait_ge(x_ready, TB + tb + 1))
            norm_turned(TR_F2, hT)
            route(1, S_WQ2)
            gates(1, 0)
            for tb in range(TB):
                for q in range(QUARTERS):
                    gelus(1, tb, q, ACT.Gelu_apprx_tanh)
                    if q == 0 and tb + 1 < TB:
                        gates(1, tb + 1)
                act.wait_ge(acc_done, TB + tb + 1)
                steps.inc(act.activation(xn[:, tb, :].rearrange("p (k n) -> p k n", k=2), obk[:, :, :], ACT.Square,
                                         accum_out=ss[:, tb:tb + 1]))
                steps.wait()
                root(rstd[:, tb:tb + 1], ss[:, tb:tb + 1], D, rms_done)

        @block.vector
        def _(v):
            steps = Count(v, vec)

            def link(ins):
                steps.inc(ins)
                steps.wait()

            def bcast(t, axis, shape):
                return t.unsqueeze(axis).to_broadcast(shape)

            v.memset(epsc, EPS).then_inc(vec, 1)
            steps.n += 1
            v.memset(zeros[:, 0:128], 0.0).then_inc(mm_free, 4)
            v.memset(zeros[:, 128:256], 0.0).then_inc(key_done, 4)
            v.memset(zeros[:, 256:384], 0.0).then_inc(key_free, 4)
            v.memset(zeros[:, 384:512], 0.0).then_inc(acc_free, 1)
            v.memset(zeros[:, 512:640], 0.0).then_inc(slot_free, RING)
            v.memset(dots[:, :], 0.0).then_inc(zeros_set, 1)

            def inverse_rms(n):
                v.wait_ge(rms_done, n)
                link(v.reciprocal(rstd, rstd))

            v.wait_ge(in_g1, 16)
            inverse_rms(1)
            for tb in range(TB):
                v.scalar_tensor_tensor(xn[:, tb, :], x_res[:, tb, :], rstd[:, tb:tb + 1], gain1,
                                       ALU.mult, ALU.mult).then_inc(xn_ready, 1)

            def rotate(n, s, src, half, cos, sin):
                v.wait_ge(mm_free, 4 * (s + 1) + 4)
                x = stg[:, src, :, :].rearrange("p b (h e) -> p b h e", e=QK)
                x1, x2 = x[:, :, :, 0:half], x[:, :, :, half:2 * half]
                shape = [P, TB, 8, half]
                t = [rtmp[:, k, 0:TB * 8 * half].rearrange("p (b h e) -> p b h e", b=TB, h=8) for k in range(4)]
                c, s_ = bcast(cos, 2, shape), bcast(sin, 2, shape)
                for k, (a, b) in enumerate(((x1, c), (x2, s_), (x2, c), (x1, s_))):
                    i = v.tensor_tensor(t[k], a, b, ALU.mult)
                link(i)
                v.tensor_tensor(x1, t[0], t[1], ALU.subtract)
                v.tensor_tensor(x2, t[2], t[3], ALU.add).then_inc(rotated, 1)
                v.wait_ge(rotated, n + 1)

            v.wait_ge(in_blk1, 16 * 8)
            rotate(0, 0, 0, 8, cosd, sind)
            rotate(1, 1, 1, 8, cosd, sind)
            rotate(2, 3, 0, 32, cosr, sinr)

            for m in range(2):
                i = v.scalar_tensor_tensor(rtmp[:, m, 0:QK], lamp[:, 2 * m * QK:(2 * m + 1) * QK], 1.0,
                                           lamp[:, (2 * m + 1) * QK:(2 * m + 2) * QK], ALU.mult, ALU.mult,
                                           accum_out=lam[:, m:m + 1])
                if m:
                    i.then_inc(lam_arg, 1)
            v.wait_ge(lam_exp, 2)
            v.scalar_tensor_tensor(lam[:, 0:1], lam[:, 3:4], LAMBDA_INIT, lam[:, 2:3], ALU.subtract, ALU.subtract)
            link(v.tensor_scalar(lgam, lgam, -1.0, None, ALU.mult))
            for h in range(H):
                link(v.tensor_scalar(decay[:, h, :], dist[:, 0, :], lgam[:, h:h + 1], None, ALU.mult))
                v.scalar_tensor_tensor(decay[:, h, :], dist[:, 1, :], lgam[:, H + h:H + h + 1], decay[:, h, :],
                                       ALU.mult, ALU.add).then_inc(dec_arg, 1)

            def maxima(n):
                v.wait_ge(sc_done, n + 1)
                if n >= 2:
                    v.wait_ge(sc_exp, n - 1)
                link(v.tensor_reduce(mx[:, n % 2, :], proj[:, 2 * (n % 2):2 * (n % 2) + 2, :], AX, ALU.max))
                v.tensor_scalar(nmx[:, n % 2, :], mx[:, n % 2, :], -QK ** -0.5, None, ALU.mult).then_inc(sc_max, 1)

            def mixed(n):
                k = n % 2
                v.wait_ge(sc_exp, n + 1)
                link(v.reciprocal(pinv[:, k, :], psum[:, k, :]))
                link(v.tensor_scalar(pinv[:, k, 1:2], pinv[:, k, 1:2], lam[:, 0:1], None, ALU.mult))
                if n >= 2:
                    v.wait_ge(tr_done, TR_A + n - 1)
                link(v.tensor_scalar(atile[:, k, :], prob[:, k, 0, :], pinv[:, k, 0:1], None, ALU.mult))
                v.scalar_tensor_tensor(atile[:, k, :], prob[:, k, 1, :], pinv[:, k, 1:2], atile[:, k, :],
                                       ALU.mult, ALU.add).then_inc(a_ready, 1)

            for n in range(H * TB + 1):
                if n < H * TB:
                    maxima(n)
                if n:
                    mixed(n - 1)

            for h in range(H):
                v.wait_ge(dec_done, h + 1)
                if h >= 2:
                    v.wait_ge(o_done, H * TB + h - 1)
                for j in range(TB):
                    v.wait_ge(rs_done, TB * h + j + 1)
                    at = (TB - 1 - j) * P
                    v.scalar_tensor_tensor(rP[:, h % 2, j, :], proj[:, j, :], QK ** -0.5, decay[:, h, at:at + T],
                                           ALU.mult, ALU.mult).then_inc(rp_ready, 1)

            full = [P, TB, H, P]
            a = xn[:, :, 0:512].rearrange("p b (h n) -> p b h n", h=H)
            r = xn[:, :, 512:1024].rearrange("p b (h n) -> p b h n", h=H)
            v.wait_ge(o_free, H * TB)
            link(v.tensor_tensor(sq16, a, a, ALU.mult))
            v.tensor_reduce(st16, sq16, AX, ALU.add).then_inc(hn_arg, 1)
            v.wait_ge(hn_done, 1)
            link(v.reciprocal(st16, st16))
            link(v.tensor_scalar(st16, st16, 1.0 - LAMBDA_INIT, None, ALU.mult))
            link(v.tensor_tensor(a, a, bcast(st16, 3, full), ALU.mult))
            link(v.tensor_tensor(a, a, diffg.unsqueeze(1).unsqueeze(1).to_broadcast(full), ALU.mult))
            v.wait_ge(o_free, H * TB + H)
            link(v.tensor_reduce(st16, r, AX, ALU.add))
            link(v.tensor_scalar(st16, st16, 1.0 / P, None, ALU.mult))
            link(v.tensor_tensor(r, r, bcast(st16, 3, full), ALU.subtract))
            link(v.tensor_tensor(sq16, r, r, ALU.mult))
            v.tensor_reduce(sv16, sq16, AX, ALU.add).then_inc(hn_arg, 1)
            v.wait_ge(hn_done, 2)
            link(v.reciprocal(sv16, sv16))
            link(v.tensor_tensor(r, r, bcast(sv16, 3, full), ALU.mult))
            link(v.tensor_tensor(xn[:, :, 512:1024], xn[:, :, 512:1024], bcast(retg, 1, [P, TB, 512]), ALU.mult))
            v.tensor_tensor(xn[:, :, 512:1024], xn[:, :, 512:1024], rg, ALU.mult).then_inc(mix_ready, 1)

            for s in range(N_OUT1):
                for tb in range(TB):
                    v.wait_ge(mm_done, 4 * (S_OUT1 + s) + tb + 1)
                    c = slice(512 * s, 512 * (s + 1))
                    v.tensor_tensor(x_res[:, tb, c], x_res[:, tb, c], proj[:, tb, :], ALU.add).then_inc(mm_free, 1)
            v.wait_ge(c_silu, 1)
            v.tensor_copy(cbc, bcast(silc, 2, [P, DC, P])).then_inc(cbc_ready, 1)
            inverse_rms(2)
            for tb in range(TB):
                v.scalar_tensor_tensor(xn[:, tb, :], x_res[:, tb, :], rstd[:, tb:tb + 1], gain2,
                                       ALU.mult, ALU.mult).then_inc(xn_ready, 1)

            LOW = -3.0e38

            def rank_keys(layer):
                for g in range(HP):
                    bank = tps if g % 4 < 2 else obk
                    s = [bank[:, g % 2, tb * P:(tb + 1) * P] for tb in range(TB)]
                    v.wait_ge(key_done, layer * HP + g + 1 + 4)
                    for tb in range(TB):
                        i = v.max(tops[:, tb, g, 0:8], s[tb])
                    link(i)
                    for tb in range(TB):
                        v.max_index(topu[:, tb, g, 0:8], tops[:, tb, g, 0:8], s[tb])
                    for tb in range(TB):
                        i = v.match_replace(srep[:, g % 2, tb, :], tops[:, tb, g, 0:8], s[tb], LOW)
                    i.then_inc(key_free, 1)
                    v.wait_ge(key_free, layer * HP + g + 1 + 4)
                    for tb in range(TB):
                        i = v.max(tops[:, tb, g, 8:16], srep[:, g % 2, tb, :])
                    link(i)
                    for tb in range(TB):
                        i = v.max_index(topu[:, tb, g, 8:16], tops[:, tb, g, 8:16], srep[:, g % 2, tb, :])
                link(i)
                link(v.tensor_copy(topi, topu))

            grid = [P, PH, K, K]

            def choose(layer, tb):
                s = tops[:, tb, :, :].rearrange("p (h c) k -> p h c k", c=2)
                link(v.tensor_tensor(cand, bcast(s[:, :, 0, :], 3, grid), bcast(s[:, :, 1, :], 2, grid), ALU.add))
                c = cand.rearrange("p h i j -> p h (i j)")
                for h in range(PH):
                    i = v.max(best[:, h, 0:8], c[:, h, :])
                link(i)
                for h in range(PH):
                    v.max_index(posu[:, h, 0:8], best[:, h, 0:8], c[:, h, :])
                for h in range(PH):
                    i = v.match_replace(cand2[:, h, :], best[:, h, 0:8], c[:, h, :], LOW)
                link(i)
                for h in range(PH):
                    i = v.max(best[:, h, 8:16], cand2[:, h, :])
                link(i)
                for h in range(PH):
                    i = v.max_index(posu[:, h, 8:16], best[:, h, 8:16], cand2[:, h, :])
                v.tensor_tensor(expg, best, best[:, :, 0:1].to_broadcast([P, PH, K]), ALU.subtract).then_inc(g_arg, 1)
                v.wait_ge(g_arg, layer * TB + tb + 1)

            def key_numbers(tb, m):
                ids = topi[:, tb, :, :].rearrange("p (h c) k -> p h c k", c=2)
                op, arg = ((ALU.logical_shift_right, 4), (ALU.bitwise_and, 15))[m]
                link(v.tensor_single_scalar(half_u, posu, arg, op))
                link(v.tensor_copy(half_f, half_u))
                link(v.tensor_tensor(onehot, bcast(half_f, 3, grid), iota[:, :].unsqueeze(1).unsqueeze(1).to_broadcast(grid),
                                     ALU.is_equal))
                link(v.tensor_tensor(onehot, onehot, bcast(ids[:, :, m, :], 2, grid), ALU.mult))
                link(v.tensor_reduce(idf[:, m, :, :], onehot, AX, ALU.add))

            def experts(layer, tb):
                at = slice(tb * SLOTS, (tb + 1) * SLOTS)
                v.scalar_tensor_tensor(eid[:, at].rearrange("p (h k) -> p h k", h=PH), idf[:, 0, :, :], float(NK), idf[:, 1, :, :],
                                       ALU.mult, ALU.add).then_inc(eid_ready, 1)
                v.wait_ge(g_exp, layer * TB + tb + 1)
                link(v.tensor_reduce(gsum, expg, AX, ALU.add))
                link(v.reciprocal(gsum, gsum))
                link(v.tensor_tensor(gate[:, at].rearrange("p (h k) -> p h k", h=PH), expg, bcast(gsum, 2, [P, PH, K]), ALU.mult))

            def route(layer, tb):
                choose(layer, tb)
                key_numbers(tb, 0)
                key_numbers(tb, 1)
                experts(layer, tb)

            def expert_dots(layer, tb, q):
                with v.Fori(0, QSLOTS // RING) as it:
                    n = ((layer * TB + tb) * SLOTS + q * QSLOTS) // RING
                    for g in range(RING // GROUP):
                        gs = slice(g * GROUP, (g + 1) * GROUP)
                        for r_ in range(g * GROUP, (g + 1) * GROUP):
                            v.wait_ge(row[r_], it * 16 + (16 * n + 16))
                            v.scalar_tensor_tensor(rows[:, r_, 0:D], rows[:, r_, 0:D], 1.0, xn[:, tb, :], ALU.mult, ALU.mult,
                                                   accum_out=dots[:, r_:r_ + 1]).then_inc(dot_done, 1)
                        v.wait_ge(gelu_done, it * (RING // GROUP) + (n * (RING // GROUP) + g + 1))
                        v.tensor_tensor(coef[:, gs], gelu[:, gs], gate[:, bass.ds(it * RING + (tb * SLOTS + q * QSLOTS + g * GROUP), GROUP)],
                                        ALU.mult).then_inc(coef_done, 1)
                        v.wait_ge(coef_done, it * (RING // GROUP) + (n * (RING // GROUP) + g + 1))
                        for r_ in range(g * GROUP, (g + 1) * GROUP):
                            v.wait_ge(slot_free, it * RING + (RING * n + r_ + 1))
                            v.tensor_scalar(diag[:, r_, :], ident[:, :], coef[:, r_:r_ + 1], None,
                                            ALU.mult).then_inc(diag_ready, 1)

            def modulation(n):
                v.wait_ge(in_bias, 16)
                flat = ada[:, :, :].rearrange("p k n -> p (k n)")
                v.wait_ge(mm_done, 4 * (S_ADA + n + 1))
                c = slice(512 * n, 512 * (n + 1))
                v.tensor_tensor(flat[:, c], flat[:, c], proj[:, n % 4, :], ALU.add).then_inc(mm_free, 4)

            def between(layer, tb, q):
                if tb + 1 == TB:
                    return
                if q == 0:
                    choose(layer, tb + 1)
                elif q == 1:
                    key_numbers(tb + 1, 0)
                elif q == 2:
                    key_numbers(tb + 1, 1)
                    experts(layer, tb + 1)

            rank_keys(0)
            route(0, 0)
            for tb in range(TB):
                for q in range(QUARTERS):
                    if q < N_ADA // TB:
                        modulation(tb * (N_ADA // TB) + q)
                    expert_dots(0, tb, q)
                    between(0, tb, q)
                v.wait_ge(acc_done, tb + 1)
                v.tensor_tensor(x_res[:, tb, :].rearrange("p (k n) -> p k n", k=2),
                                x_res[:, tb, :].rearrange("p (k n) -> p k n", k=2), obk[:, :, :], ALU.add).then_inc(acc_free, 1)

            v.wait_ge(in_late, 32)
            inverse_rms(3)
            for tb in range(TB):
                v.scalar_tensor_tensor(x_res[:, tb, :], x_res[:, tb, :], rstd[:, tb:tb + 1], late[:, 0, :],
                                       ALU.mult, ALU.mult).then_inc(x_ready, 1)
            v.wait_ge(mm_free, 4 * S_CONV + 4)
            link(v.scalar_tensor_tensor(ada[:, 1, :], ada[:, 1, :], 1.0, late[:, 1, :], ALU.add, ALU.mult))

            def modulated(scale, shift):
                for tb in range(TB):
                    link(v.scalar_tensor_tensor(xn[:, tb, :], x_res[:, tb, :], rstd[:, tb:tb + 1], ada[:, scale, :],
                                                ALU.mult, ALU.mult))
                    v.tensor_tensor(xn[:, tb, :], xn[:, tb, :], ada[:, shift, :], ALU.add).then_inc(xn_ready, 1)

            inverse_rms(4)
            modulated(1, 0)

            link(v.memset(cx[:, :, 0:2], 0.0))
            v.wait_ge(in_conv, 16)
            for j in range(DC):
                job, k = 4 * S_CONV + 3 * j, j % 2
                v.wait_ge(c_copied, j + 1)
                v.wait_ge(mm_done, job + 2)
                v.tensor_tensor(cx[:, k, 2:2 + T], csb[:, k, :], proj[:, (job + 1) % 4, :], ALU.mult).then_inc(mm_free, 2)
                v.wait_ge(mm_free, job + 2 + 4)
                link(v.tensor_scalar(ctmp[:, k, :], cx[:, k, 0:T], convw[:, 3 * j:3 * j + 1], None, ALU.mult))
                for t in (1, 2):
                    link(v.scalar_tensor_tensor(ctmp[:, k, :], cx[:, k, t:t + T], convw[:, 3 * j + t:3 * j + t + 1],
                                                ctmp[:, k, :], ALU.mult, ALU.add))
                v.wait_ge(mm_done, job + 3)
                v.tensor_tensor(yaT[:, j, :], ctmp[:, k, :], proj[:, (job + 2) % 4, :], ALU.mult).then_inc(mm_free, 1)

            v.wait_ge(mm_free, 4 * S_QK2 + 4)
            v.memset(cx[:, :, 0:3], 0.0).then_inc(qk_conv, 1)
            for j in range(N_QK * 4):
                k, w = j % 2, 24 + 4 * j
                v.wait_ge(mm_free, 4 * S_QK2 + j + 1 + 4)
                if j >= 2:
                    v.wait_ge(qk_ready, j - 1)
                link(v.tensor_scalar(ctmp[:, k, :], cx[:, k, 0:T], convw[:, w:w + 1], None, ALU.mult))
                for t in (1, 2, 3):
                    i = v.scalar_tensor_tensor(ctmp[:, k, :], cx[:, k, t:t + T], convw[:, w + t:w + t + 1],
                                               ctmp[:, k, :], ALU.mult, ALU.add)
                    if t < 3:
                        link(i)
                    else:
                        i.then_inc(qk_conv, 1)
            v.memset(vaug[:, :, :, P:P + 1], 1.0).then_inc(v_ones, 1)

            v.wait_ge(in_lstm, 16 * 4)
            v.wait_ge(if_done, 1)
            g = [mrow[0:MH, k, :] for k in range(5)]
            v.tensor_scalar(g[2], obk[0:MH, 0, :], bif[:, 0:1], None, ALU.add)
            link(v.tensor_scalar(g[1], obk[0:MH, 1, :], bif[:, 1:2], None, ALU.add))
            v.memset(dots[:, :], 0.0).then_inc(if_act, 1)
            v.wait_ge(ln_done, 1)
            link(v.scalar_tensor_tensor(g[1], g[1], 0.0, g[0], ALU.min, ALU.subtract))
            link(v.memset(g[0], 1.0))
            link(v.tensor_tensor_scan(g[4], g[0], g[1], 0.0, ALU.mult, ALU.add))
            link(v.tensor_tensor(g[2], g[2], g[4], ALU.subtract))
            link(v.tensor_tensor_scan(g[3], g[2], g[2], 0.0, ALU.max, ALU.max))
            link(v.tensor_tensor(g[4], g[4], g[3], ALU.add))
            v.tensor_scalar(g[3], g[3], -1.0, None, ALU.mult).then_inc(if_act, 1)

            def weight_arg(n):
                h, s = divmod(n, TB)
                v.wait_ge(nm_done, h + 1)
                if n >= 2:
                    v.wait_ge(p_ready, n - 1)
                v.tensor_scalar(wts[:, n % 2, s * P:T], tps[:, h % 2, s * P:T], acol[:, s, h:h + 1], 0.0,
                                ALU.add, ALU.min).then_inc(w_arg, 1)

            def weighted(n):
                h, s = divmod(n, TB)
                at = sum(T - P * u for u in range(s))
                if h >= 2 and s == 0:
                    v.wait_ge(num_done, h - 1)
                v.wait_ge(rs_done, H * TB + n + 1)
                v.wait_ge(w_exp, n + 1)
                link(v.scalar_tensor_tensor(mP[:, h % 2, at:at + T - s * P], proj[:, s, s * P:T], QK ** -0.5,
                                            wts[:, n % 2, s * P:T], ALU.mult, ALU.mult))
                dg = mP[:, h % 2, at:at + P]
                v.tensor_tensor(dg, dg, tri[:, :], ALU.mult).then_inc(p_ready, 1)

            nums = obk[:, :, :].rearrange("p k (e n) -> p (k e) n", e=2)

            def head_out(h):
                v.wait_ge(num_done, h + 1)
                dn = nums[:, :, P:P + 1].rearrange("p b n -> p (b n)")
                link(v.tensor_scalar(den, dn, -1.0, None, ALU.mult))
                link(v.tensor_tensor(den, den, dn, ALU.max))
                link(v.tensor_tensor(den, den, ecol[:, :, h], ALU.max))
                link(v.reciprocal(dinv, den))
                v.tensor_tensor(hm[:, :, h, :], nums[:, :, 0:P], bcast(dinv, 2, [P, TB, P]), ALU.mult).then_inc(num_free, 1)

            v.wait_ge(cols_ready, 2)
            for n in range(MH * TB + 1):
                if n < MH * TB:
                    weight_arg(n)
                if n:
                    weighted(n - 1)
                    if n % TB == 0 and n > TB:
                        head_out(n // TB - 2)
            head_out(MH - 1)

            v.wait_ge(num_free, MH)
            x32 = xn[:, :, :].rearrange("p b (h n) -> p b h n", h=MH)
            link(v.tensor_tensor(x32, hm, hm, ALU.mult))
            v.tensor_reduce(st32, x32, AX, ALU.add).then_inc(hn_arg, 1)
            v.wait_ge(hn_done, 3)
            link(v.reciprocal(st32, st32))
            link(v.tensor_tensor(hm, hm, bcast(st32, 3, [P, TB, MH, P]), ALU.mult))
            v.wait_ge(in_mhg, 16)
            link(v.tensor_tensor(hmw, hmw, bcast(mhg, 1, [P, TB, D]), ALU.mult))
            for n in range(N_O * TB):
                s, tb = divmod(n, TB)
                c = slice(512 * s, 512 * (s + 1))
                v.wait_ge(mm_free, 4 * S_O2 + n + 1 + 4)
                v.tensor_tensor(hmw[:, tb, c], hmw[:, tb, c], sig[:, n % 4, :], ALU.mult).then_inc(ym_part, 1)

            for n in range(2 * DC):
                j, m = divmod(n, 2)
                v.wait_ge(g_sig, n + 1)
                v.wait_ge(mm_done, 4 * S_BR + 2 * n + 2)
                if n >= 4:
                    v.wait_ge(mixT_ready, (n - 4) // 2 + 1)
                v.tensor_tensor(sig[:, n % 4, :] if m else br1[:, j % 2, :], sig[:, n % 4, :], proj[:, (2 * n + 1) % 4, :],
                                ALU.mult).then_inc(mm_free, 2)
                if m:
                    v.wait_ge(mm_free, 4 * S_BR + 2 * n + 2 + 4)
                    v.tensor_tensor(mixT[:, j, :], br1[:, j % 2, :], sig[:, n % 4, :], ALU.add).then_inc(mixT_ready, 1)

            v.wait_ge(in_post, 16 * 3)
            v.tensor_tensor(ada[:, 2, :], ada[:, 2, :], post[:, 0, :], ALU.mult)
            v.scalar_tensor_tensor(ada[:, 4, :], ada[:, 4, :], 1.0, post[:, 1, :], ALU.add, ALU.mult)
            link(v.tensor_tensor(ada[:, 5, :], ada[:, 5, :], post[:, 2, :], ALU.mult))
            inverse_rms(5)
            for tb in range(TB):
                link(v.scalar_tensor_tensor(hmw[:, tb, :], hmw[:, tb, :], rstd[:, tb:tb + 1], ada[:, 2, :], ALU.mult, ALU.mult))
                v.tensor_tensor(x_res[:, tb, :], x_res[:, tb, :], hmw[:, tb, :], ALU.add).then_inc(x_ready, 1)
            inverse_rms(6)
            modulated(4, 3)

            rank_keys(1)
            route(1, 0)
            for tb in range(TB):
                for q in range(QUARTERS):
                    expert_dots(1, tb, q)
                    between(1, tb, q)
                v.wait_ge(rms_done, 7 + tb)
                link(v.reciprocal(rstd[:, tb:tb + 1], rstd[:, tb:tb + 1]))
                y = xn[:, tb, :].rearrange("p (k n) -> p k n", k=2)
                v.scalar_tensor_tensor(y, obk[:, :, :], rstd[:, tb:tb + 1], ada[:, 5, :].rearrange("p (k n) -> p k n", k=2),
                                       ALU.mult, ALU.mult).then_inc(acc_free, 1)
                v.wait_ge(acc_free, TB + tb + 2)
                v.tensor_tensor(x_res[:, tb, :], x_res[:, tb, :], xn[:, tb, :], ALU.add).then_inc(out_ready, 1)


def by_rows(w):
    return w.reshape(DC, P, -1, 512).transpose(2, 1, 0, 3).reshape(-1, P, SLAB)


def by_tiles(tiles):
    t = np.stack(tiles).reshape(-1, 4, DC, P, P)
    return t.transpose(0, 3, 1, 2, 4).reshape(-1, P, SLAB)


def columns(w):
    return [w[:, c:c + P] for c in range(0, w.shape[1], P)]


def broad(a):
    return np.ascontiguousarray(np.broadcast_to(np.reshape(a, (1, -1)), (P, np.size(a))))


def constants():
    pos = np.arange(T, dtype=np.float32)
    fd = np.power(np.float32(500000.0), -np.arange(8, dtype=np.float32) * np.float32(2.0) / np.float32(16))
    fr = np.float32(1.0) / np.power(np.float32(10000.0), np.linspace(0.0, 1.0, 32, dtype=np.float32))
    rope = []
    for f in (fd, fr):
        ang = (pos[:, None] * f[None, :].astype(np.float32)).astype(np.float32)
        for fn in (np.cos, np.sin):
            rope.append(fn(ang).astype(np.float32).reshape(TB, P, -1).transpose(1, 0, 2).reshape(P, -1))
    away = np.arange(2 * T - P, dtype=np.float32)[None, :] - (T - P) - np.arange(P, dtype=np.float32)[:, None]
    sel = np.zeros((MH, MH, P), np.float32)
    sel[np.arange(MH), np.arange(MH)] = 1.0
    return {
        "rope": np.concatenate(rope, axis=1),
        "dist": np.concatenate([np.maximum(away, 0), np.maximum(-away, 0)], axis=1),
        "ident": np.eye(P, dtype=np.float32),
        "tri": np.triu(np.ones((P, P), np.float32)),
        "iota": np.ascontiguousarray(np.broadcast_to(np.arange(K, dtype=np.float32), (P, K))),
        "sel": sel,
    }


def lay_out(inp):
    a = {k: np.asarray(v) for k, v in inp.items()}
    w2 = a["w_in_2"][0]
    cuts = np.cumsum([1024, 1024, 1024, 512, 512, 1024, 1024, 8, 8, 1024])
    cg, bg, xi, q, k, v, o, ig, fg, ga, gm = np.split(w2, cuts, axis=1)
    conv = [t for c, x, b in zip(columns(cg), columns(xi), columns(bg)) for t in (c, x, b)]
    br = [t for g1, wa, g2, wm in zip(columns(ga), columns(a["w_branch_a_2"][0]), columns(gm), columns(a["w_branch_m_2"][0]))
          for t in (g1, wa, g2, wm)]
    slabs = np.concatenate([
        by_rows(a["w_in"][0]), by_rows(a["w_out"][0]), by_tiles(columns(a["peer_w_query"][0])), by_rows(a["w_ada_2"][0]),
        by_tiles(conv), by_tiles(columns(q) + columns(k)), by_rows(v), by_rows(o), by_tiles(br), by_rows(a["w_out_2"][0]),
        by_tiles(columns(a["peer_wq_2"][0]))])
    d = constants()
    d.update(
        x=a["x"][0], slabs=slabs, c_2=np.ascontiguousarray(a["c_2"].reshape(DC, P).T),
        experts1=np.concatenate([a["peer_u"][0], a["peer_v"][0]], axis=1),
        experts2=np.concatenate([a["peer_u_2"][0], a["peer_v_2"][0]], axis=1),
        keys1=np.ascontiguousarray(a["peer_sub_keys"][0].reshape(HP, NK, P).transpose(2, 0, 1)),
        keys2=np.ascontiguousarray(a["peer_subkeys_2"][0].reshape(HP, NK, P).transpose(2, 0, 1)),
        b_ada_2=broad(a["b_ada_2"]).reshape(P, 6, D),
        conv_w=np.ascontiguousarray(np.concatenate([
            a["conv_a_w_2"][0].reshape(3, DC, P).transpose(2, 1, 0).reshape(P, -1),
            a["conv_qk_w_2"][0].reshape(4, DC, P).transpose(2, 1, 0).reshape(P, -1)], axis=1)),
        b_if=np.ascontiguousarray(np.stack([a["b_igate_2"][0], a["b_fgate_2"][0]], axis=1)),
        w_if=np.ascontiguousarray(np.concatenate([ig, fg], axis=1).reshape(DC, P, 2 * MH).transpose(1, 0, 2)),
    )
    for n in ("attn_norm_g", "diff_norm_g", "ret_norm_g", "diff_lambda", "ret_log_decay", "ffn_norm_g", "final_norm_g",
              "norm1_pre_2", "norm1_post_2", "norm2_pre_2", "norm2_post_2", "mh_norm_w_2"):
        d[n] = broad(a[n])
    return {k: np.ascontiguousarray(t, dtype=np.float32) for k, t in d.items()}


def kernel(**inputs):
    import concourse.bacc as bacc
    from concourse.bass_utils import run_bass_kernel_spmd

    arrays = lay_out(inputs)
    nc = bacc.Bacc("TRN2", target_bir_lowering=False, num_devices=1)
    d = {n: nc.dram_tensor(f"in_{n}", t.shape, F32, kind="ExternalInput").ap() for n, t in arrays.items()}
    out = nc.dram_tensor("out", (T, D), F32, kind="ExternalOutput").ap()
    build(nc, d, out)
    got = run_bass_kernel_spmd(nc, [{f"in_{n}": t for n, t in arrays.items()}], core_ids=[0])
    return got.results[0]["out"].reshape(1, T, D)
```

```python
from contextlib import ExitStack

import numpy as np

import concourse.bass as bass
from concourse import mybir

F32 = mybir.dt.float32
BF16 = mybir.dt.bfloat16
U32 = mybir.dt.uint32
ALU = mybir.AluOpType
ACT = mybir.ActivationFunctionType
AX = mybir.AxisListType.X

P = 128
D = 1024
T = 512
TB = T // P
DC = D // P
EPS = 1e-6
H = 4
QK = 64
LAMBDA_INIT = 0.2
MH = 8
PH = 8
HP = 2 * PH
NK = 128
K = 16
SLOTS = PH * K
PAIR = 2
SLAB = DC * 512

GB = 2
RING = 6
GROUP = RING // 2
UNITS, TAIL = divmod(GB * SLOTS, RING)
GROUPS = 2 * UNITS + 1
ROUTED = 2
EARLY = 10
DT = (TB - GB) * P
TILES = NK
BODY = 4
CK = 32
CHUNKS = NK // CK
STEPS = CK // BODY
SG = 4
SGROUPS = DT // SG
ROUNDS = 4
assert EARLY - ROUTED == 2 * ROUNDS
RGROUPS = SGROUPS // ROUNDS
RTILES = CK // ROUNDS
assert RTILES == 4 * PAIR and RGROUPS == 2 * RTILES
HOT2 = RGROUPS * ROUNDS // 2 + (CHUNKS - 1) * SGROUPS
assert EARLY + CHUNKS * STEPS == UNITS and SGROUPS == 2 * BODY * STEPS

N_IN1, N_OUT1, N_WQ, N_ADA, N_EXP, N_CONV, N_QK, N_V, N_O, N_BR, N_OUT2 = 6, 2, 4, 12, TILES // 2, 6, 2, 2, 2, 8, 2
S_IN1 = 0
S_OUT1 = S_IN1 + N_IN1
S_WQ1 = S_OUT1 + N_OUT1
S_ADA = S_WQ1 + N_WQ
S_EXP1 = S_ADA + N_ADA
S_CONV = S_EXP1 + N_EXP
S_QK2 = S_CONV + N_CONV
S_V2 = S_QK2 + N_QK
S_O2 = S_V2 + N_V
S_BR = S_O2 + N_O
S_OUT2 = S_BR + N_BR
S_WQ2 = S_OUT2 + N_OUT2
S_EXP2 = S_WQ2 + N_WQ
N_SLABS = S_EXP2 + N_EXP


class Count:

    def __init__(self, eng, sem):
        self.eng, self.sem, self.n = eng, sem, 0

    def inc(self, ins):
        self.n = self.n + 1
        return ins.then_inc(self.sem, 1)

    def wait(self):
        self.eng.wait_ge(self.sem, self.n)


def build(nc, d, out):
    with ExitStack() as ctx:
        def sb(name, shape, dt=F32):
            return ctx.enter_context(nc.sbuf_tensor(name, shape, dt))

        def ps(name, shape):
            return ctx.enter_context(nc.psum_tensor(name, shape, F32))

        def sem(name):
            return ctx.enter_context(nc.semaphore(name))

        x_res = sb("x_res", [P, TB, D])
        xn = sb("xn", [P, TB, D])
        hT = sb("hT", [P, DC, T])
        wring = sb("wring", [P, PAIR, SLAB])
        NRING, NSPREAD = RING * 2 * D, 2 * DT * CK
        ring = sb("ring", [P, NRING + NSPREAD])
        ident = sb("ident_sb", [P, P])
        tri = sb("tri_sb", [P, P])
        iota = sb("iota_sb", [P, NK])
        zeros = sb("zeros", [1, P + 512], BF16)
        stat = sb("stat", [P, 192])
        eid = sb("eid", [P, SLOTS, GB], U32)
        gate = sb("gate", [P, SLOTS, GB])
        table = sb("table", [P, 4, DT])
        hot2 = sb("hot2", [P, 2, SG, NK])
        idx = sb("idx", [P, 2, RING], U32)
        dots = sb("dots", [P, RING])
        gelu = sb("gelu", [P, RING])
        coef = sb("coef", [P, RING])

        proj = ps("proj", [P, 4, 512])
        tps = ps("tps", [P, 2, 512])
        obk = ps("obk", [P, 2, 512])

        def part(t, at, n):
            return t[:, at:at + n]

        rows = part(ring, 0, NRING).rearrange("p (r n) -> p r n", r=RING)
        spread = part(ring, NRING, NSPREAD).rearrange("p (k t n) -> p k t n", k=2, t=DT)
        work = part(ring, 16384, 8192)
        gathered = xn[:, GB:2 * GB, :]
        act_z = hT[:, 0:2, 0:DT]
        coef_t = hT[:, 2:4, 0:DT]
        first_z = part(ring, NRING + NSPREAD // 2, CK * DT).rearrange("p (i t) -> p i t", t=DT)
        hot1 = hT[:, 4, 0:2 * SG * CK].rearrange("p (k t n) -> p k t n", k=2, t=SG)

        dqT = part(ring, 0, 2048).rearrange("p (c t) -> p c t", c=4)
        dkT = part(ring, 2048, 2048).rearrange("p (c t) -> p c t", c=4)
        rqkT = part(ring, 4096, 2048).rearrange("p (c t) -> p c t", c=4)
        dv = part(ring, 6144, 2048).rearrange("p (b n) -> p b n", b=TB)
        rv = part(ring, 8192, 2048).rearrange("p (b n) -> p b n", b=TB)
        rg = part(ring, 10240, 2048).rearrange("p (b n) -> p b n", b=TB)
        NTOE = 2 * T - P
        decay = part(ring, 12288, H * NTOE).rearrange("p (h n) -> p h n", h=H)
        rope = part(ring, 15872, 320)
        cosd = part(rope, 0, 32).rearrange("p (b n) -> p b n", b=TB)
        sind = part(rope, 32, 32).rearrange("p (b n) -> p b n", b=TB)
        cosr = part(rope, 64, 128).rearrange("p (b n) -> p b n", b=TB)
        sinr = part(rope, 192, 128).rearrange("p (b n) -> p b n", b=TB)
        stg = xn[:, :, :].rearrange("p b n -> p (b n)").rearrange("p (s b n) -> p s b n", s=2, b=TB)
        gain1 = part(work, 0, D)
        gain2 = part(ring, 26624, D)
        rtmp = part(work, 1024, 4096).rearrange("p (k n) -> p k n", k=4)
        dist = part(work, 5120, 2 * NTOE).rearrange("p (k n) -> p k n", k=2)
        diffg = part(ring, 24576, P)
        retg = part(ring, 24576 + P, H * P)
        lamp = part(ring, 25600, 4 * QK)
        rdec = part(ring, 25856, 8)
        prob = part(work, 0, 2048).rearrange("p (k m n) -> p k m n", k=2, m=2)
        atile = part(work, 2048, 1024).rearrange("p (k n) -> p k n", k=2)
        aT = part(work, 3072, 1024).rearrange("p (k n) -> p k n", k=2)
        rP = part(work, 4096, 4096).rearrange("p (k j n) -> p k j n", k=2, j=TB)
        sq16 = part(work, 0, 2048).rearrange("p (b h n) -> p b h n", b=TB, h=H)

        subk = part(ring, 0, HP * NK).rearrange("p (g n) -> p g n", g=HP)
        qT = part(ring, 2048, 2048).rearrange("p (k t) -> p k t", k=4)
        srep = part(ring, 4096, 1024).rearrange("p (k b n) -> p k b n", k=2, b=TB)
        topu = part(ring, 5120, 1024).bitcast(U32).rearrange("p (b g k) -> p b g k", b=TB, g=HP)
        LONG, SHORT = 4, 4
        NCAND = LONG * K + (K - LONG) * SHORT
        cand = part(ring, NRING, PH * NCAND).rearrange("p (h n) -> p h n", h=PH)
        cand2 = part(ring, NRING + 2048, PH * NCAND).rearrange("p (h n) -> p h n", h=PH)
        onehot = part(ring, NRING + 2048, 2048).rearrange("p (h k j) -> p h k j", h=PH, k=K)
        tops = part(ring, NRING + 4096, 1024).rearrange("p (b g k) -> p b g k", b=TB, g=HP)
        topi = part(ring, NRING + 5120, 1024).rearrange("p (b g k) -> p b g k", b=TB, g=HP)
        small = part(ring, NRING + 6144, 1024)
        idf = part(small, 0, 256).rearrange("p (c h k) -> p c h k", c=2, h=PH)
        expg = part(small, 256, 128).rearrange("p (h k) -> p h k", h=PH)
        best = part(small, 512, 128).rearrange("p (h k) -> p h k", h=PH)
        pos_row = part(small, 384, 128).rearrange("p (h k) -> p h k", h=PH)
        posu = part(small, 640, 128).bitcast(U32).rearrange("p (h k) -> p h k", h=PH)
        half_u = part(small, 768, 128).bitcast(U32).rearrange("p (h k) -> p h k", h=PH)
        half_f = part(small, 896, 128).rearrange("p (h k) -> p h k", h=PH)
        choice = part(ring, NRING + 7168, (TB - GB) * 3 * SLOTS).rearrange("p (b c n) -> p b c n", c=3, n=SLOTS)
        ada_row = ring[0:1, NRING + NSPREAD // 2:NRING + NSPREAD // 2 + 6 * D]
        late = part(ring, NRING, 2 * D).rearrange("p (k n) -> p k n", k=2)
        mod1 = part(ring, NRING + 2 * D, 2 * D).rearrange("p (k n) -> p k n", k=2)
        mod2 = part(ring, 24576, 3 * D).rearrange("p (k n) -> p k n", k=3)

        vaug = part(ring, 0, TB * MH * (P + 1)).rearrange("p (b h n) -> p b h n", b=TB, h=MH)
        yaT = part(ring, 4128, 4096).rearrange("p (c t) -> p c t", c=DC)
        qT2 = part(ring, 8224, 2048).rearrange("p (c t) -> p c t", c=4)
        kT2 = part(ring, 10272, 2048).rearrange("p (c t) -> p c t", c=4)
        mixT = part(ring, 8224, 4096).rearrange("p (c t) -> p c t", c=DC)
        ymT = part(ring, 0, 4096).rearrange("p (c t) -> p c t", c=DC)
        NPT = sum(T - P * s for s in range(TB))
        mP = part(ring, 12320, 2 * NPT).rearrange("p (k n) -> p k n", k=2)
        wts = part(ring, 12320 + 2 * NPT, 1024).rearrange("p (k n) -> p k n", k=2)
        convw = part(ring, NRING + NSPREAD - 64, 56)
        hm = part(work, 0, 4096).rearrange("p (b h n) -> p b h n", b=TB, h=MH)
        hmw = part(work, 0, 4096).rearrange("p (b n) -> p b n", b=TB)
        mrow = part(work, 4096, 2560).rearrange("p (k t) -> p k t", k=5)
        sel = part(work, 6656, MH * P).rearrange("p (h m) -> p h m", h=MH)
        cx = part(work, 0, 2 * 516).rearrange("p (k n) -> p k n", k=2)
        csb = part(work, 1040, 1024).rearrange("p (k n) -> p k n", k=2)
        ctmp = part(work, 2064, 1024).rearrange("p (k n) -> p k n", k=2)
        sig = part(work, 5120, 2048).rearrange("p (k n) -> p k n", k=4)
        br1 = part(work, 7168, 1024).rearrange("p (k n) -> p k n", k=2)
        mhg = part(work, 4096, D)
        post = part(work, 4096, 2 * D).rearrange("p (k n) -> p k n", k=2)
        wif = part(work, 7680, 128).rearrange("p (c n) -> p c n", c=DC)
        bif = stat[0:MH, 188:190]
        acol = part(stat, 100, 32).rearrange("p (b h) -> p b h", b=TB)
        ecol = part(stat, 132, 32).rearrange("p (b h) -> p b h", b=TB)
        ss = part(stat, 0, 4)
        rstd = part(stat, 4, 4)
        mx = part(stat, 8, 4).rearrange("p (k m) -> p k m", k=2)
        nmx = part(stat, 12, 4).rearrange("p (k m) -> p k m", k=2)
        psum = part(stat, 16, 4).rearrange("p (k m) -> p k m", k=2)
        pinv = part(stat, 20, 4).rearrange("p (k m) -> p k m", k=2)
        lam = part(stat, 24, 4)
        lgam = part(stat, 28, 8)
        st16 = part(stat, 36, 16).rearrange("p (b h) -> p b h", b=TB)
        sv16 = part(stat, 52, 16).rearrange("p (b h) -> p b h", b=TB)
        st32 = part(stat, 36, 32).rearrange("p (b h) -> p b h", b=TB)
        dinv = part(stat, 68, 4)
        den = part(stat, 72, 4)
        silc = part(stat, 76, 8)
        epsc = part(stat, 164, 1)
        ccol = part(stat, 84, 8)
        gsum = part(stat, 92, 8)

        in_x, in_cst, in_g1, in_blk1 = sem("in_x"), sem("in_cst"), sem("in_g1"), sem("in_blk1")
        in_keys, in_bias, in_late, in_conv = sem("in_keys"), sem("in_bias"), sem("in_late"), sem("in_conv")
        in_lstm, in_mhg, in_post, stored = sem("in_lstm"), sem("in_mhg"), sem("in_post"), sem("stored")
        in_mod1, in_mod2, in_last, ada_stored = sem("in_mod1"), sem("in_mod2"), sem("in_last"), sem("ada_stored")
        slab = [sem(f"slab{k}") for k in range(PAIR)]
        row = [sem(f"row{r}") for r in range(RING)]
        mm_done, mm_free = sem("mm_done"), sem("mm_free")
        tr_done, tr_free = sem("tr_done"), sem("tr_free")
        rms_done, xn_ready, x_ready = sem("rms_done"), sem("xn_ready"), sem("x_ready")
        rotated, lam_arg, lam_exp = sem("rotated"), sem("lam_arg"), sem("lam_exp")
        dec_arg, dec_done = sem("dec_arg"), sem("dec_done")
        sc_done, sc_max, sc_exp, a_ready = sem("sc_done"), sem("sc_max"), sem("sc_exp"), sem("a_ready")
        o_done, o_free, hn_arg, hn_done = sem("o_done"), sem("o_free"), sem("hn_arg"), sem("hn_done")
        rs_done, rp_ready, mix_ready = sem("rs_done"), sem("rp_ready"), sem("mix_ready")
        key_done, key_free = sem("key_done"), sem("key_free")
        g_arg, g_exp, eid_ready, idx_ready = sem("g_arg"), sem("g_exp"), sem("eid_ready"), sem("idx_ready")
        dot_done, gelu_done, coef_done = sem("dot_done"), sem("gelu_done"), sem("coef_done")
        choice_set, hot1_set, hot_ready = sem("choice_set"), sem("hot1_set"), sem("hot_ready")
        away_set, hot2_ready = sem("away_set"), sem("hot2_ready")
        spread_done, spread_free = sem("spread_done"), sem("spread_free")
        z_done, z_act, coef_t_ready = sem("z_done"), sem("z_act"), sem("coef_t_ready")
        slot_free, acc_done, acc_free = sem("slot_free"), sem("acc_done"), sem("acc_free")
        zeros_set, out_ready, paced = sem("zeros_set"), sem("out_ready"), sem("paced")
        c_silu, c_copied, qk_conv, qk_ready = sem("c_silu"), sem("c_copied"), sem("qk_conv"), sem("qk_ready")
        v_ones, if_done, if_act, ln_done = sem("v_ones"), sem("if_done"), sem("if_act"), sem("ln_done")
        rows_ready, cols_done, cols_ready, nm_done = sem("rows_ready"), sem("cols_done"), sem("cols_ready"), sem("nm_done")
        w_arg, w_exp, p_ready, num_done, num_free = (sem("w_arg"), sem("w_exp"), sem("p_ready"), sem("num_done"),
                                                     sem("num_free"))
        ym_part, g_sig, mixT_ready = sem("ym_part"), sem("g_sig"), sem("mixT_ready")
        vec, act_s = sem("vec"), sem("act_s")

        ada_dram = nc.dram_tensor("ada_rows", (1, 6 * D), F32).ap()

        def peer_sum(tb):
            return gathered[:, tb, :].rearrange("p (k n) -> p k n", k=2) if tb < GB else proj[:, 2 * (tb - GB):2 * (tb - GB) + 2, :]

        def out_row(tb):
            return hT[:, 2 * tb:2 * tb + 2, :]

        block = ctx.enter_context(nc.Block())

        TR_N1 = 0
        TR_QK = TR_N1 + 8
        TR_A = TR_QK + 12
        TR_MIX = TR_A + 16
        TR_F1 = TR_MIX + 8
        TR_T1 = TR_F1 + 8
        TR_N2 = TR_T1 + 2
        TR_YM = TR_N2 + 8
        TR_F2 = TR_YM + 8
        TR_T2 = TR_F2 + 8

        @block.sync
        def _(sp):
            sp.dma_start(x_res[:, :, :], d["x"].rearrange("(b p) n -> p b n", p=P)).then_inc(in_x, 16)
            for k in range(PAIR):
                sp.dma_start(wring[:, k, :], d["slabs"][k]).then_inc(slab[k], 16)
            with sp.Fori(1, N_SLABS // PAIR) as pair:
                for k in range(PAIR):
                    sp.wait_ge(mm_done, pair * (4 * PAIR) + (4 * k - 4))
                    sp.dma_start(wring[:, k, :], d["slabs"][bass.ds(pair * PAIR + k, 1)].rearrange("s p n -> (s p) n")).then_inc(slab[k], 16)
            with sp.Fori(0, TB) as tb:
                sp.wait_ge(out_ready, tb + 1)
                sp.dma_start(out[bass.ts(tb, P), :], x_res[:, bass.ds(tb, 1), :].rearrange("p b n -> p (b n)")).then_inc(stored, 16)
            sp.wait_ge(stored, 16 * TB)

        @block.gpsimd
        def _(pool):
            def gather(layer):
                flat = eid[:, :, :].rearrange("p s b -> p (s b)")
                pool.wait_ge(eid_ready, GB * (layer + 1))
                pool.sem_inc(paced, 1)

                def unit(u, k, n):
                    pool.tensor_copy(idx[:, k, 0:n], flat[:, bass.ds(u * RING, n)]).then_inc(idx_ready, 1)
                    pool.wait_ge(idx_ready, u + (layer * (UNITS + 1) + 1))
                    for r in range(n):
                        pool.wait_ge(slot_free, u * RING + (layer * GB * SLOTS + r + 1))
                        pool.sem_inc(paced, 1)
                        pool.indirect_dma_start(
                            rows[:, r, :], None, d[f"experts{layer + 1}"],
                            bass.IndirectOffsetOnAxis(idx[:, k, r:r + 1], 0)).then_inc(row[r], 16)

                with pool.Fori(0, UNITS // 2) as it:
                    for k in range(2):
                        unit(it * 2 + k, k, RING)
                unit(UNITS, 0, TAIL)

            gather(0)
            gather(1)

        @block.tensor
        def _(pe):
            def transposes(job, sources):
                if job >= 2:
                    pe.wait_ge(tr_free, job - 1)
                for k, s in enumerate(sources):
                    t = pe.transpose(tps[:, job % 2, k * P:(k + 1) * P], s, ident[:, :])
                t.then_inc(tr_done, 1)

            def norm_transposes(job, src, ready, count, per):
                for tb in range(TB):
                    pe.wait_ge(ready, count + per * (tb + 1))
                    for k in range(2):
                        transposes(job + 2 * tb + k, [src[:, tb, (4 * k + c) * P:(4 * k + c + 1) * P] for c in range(4)])

            def slab_landed(k, pair):
                pe.wait_ge(slab[k], pair * 16 + 16)

            def bank_free(job):
                pe.wait_ge(mm_free, job + 1)

            def token_major(first, n, lhs):
                with pe.Fori(0, n // PAIR) as it:
                    pair = it + first // PAIR
                    for k in range(PAIR):
                        slab_landed(k, pair)
                        for tb in range(TB):
                            bank_free(pair * 8 + (4 * k + tb))
                            for c in range(DC):
                                m = pe.matmul(proj[:, tb, :], lhs[:, c, tb * P:(tb + 1) * P],
                                              wring[:, k, c * 512:(c + 1) * 512], start=(c == 0), stop=(c == DC - 1))
                            m.then_inc(mm_done, 1)

            def transposed_tile(k, j, rhs):
                for c in range(DC):
                    at = (j * DC + c) * P
                    m = pe.matmul(proj[:, j, :], wring[:, k, at:at + P], rhs[:, c, :],
                                  start=(c == 0), stop=(c == DC - 1))
                m.then_inc(mm_done, 1)

            def all_read(first):
                pe.wait_ge(mm_free, 4 * first + 4)

            def transposed(first, n, rhs):
                with pe.Fori(0, n // PAIR) as it:
                    pair = it + first // PAIR
                    for k in range(PAIR):
                        slab_landed(k, pair)
                        for j in range(4):
                            bank_free(pair * 8 + (4 * k + j))
                            transposed_tile(k, j, rhs)

            pe.wait_ge(in_cst, 32)
            norm_transposes(TR_N1, xn, xn_ready, 0, 1)
            pe.wait_ge(tr_free, TR_N1 + 8)

            def turn_staged(n, src):
                pe.wait_ge(rotated, n + 1)
                for tb in range(TB):
                    transposes(TR_QK + 4 * n + tb, [stg[:, src, tb, c * P:(c + 1) * P] for c in range(4)])

            pe.wait_ge(zeros_set, 1)
            token_major(S_IN1, 4, hT)
            turn_staged(0, 0)
            turn_staged(1, 1)
            token_major(S_IN1 + 4, 2, hT)
            turn_staged(2, 0)

            units = [(h, tb) for h in range(H) for tb in range(TB)]
            pe.wait_ge(tr_free, TR_QK + 12)
            all_read(S_OUT1)

            def scores(n):
                h, tb = units[n]
                if n >= 2:
                    pe.wait_ge(sc_exp, n - 1)
                for m in range(2):
                    q = slice(QK * m, QK * m + QK)
                    s = pe.matmul(proj[:, 2 * (n % 2) + m, :], dqT[q, h, tb * P:(tb + 1) * P], dkT[q, h, :],
                                  start=True, stop=True)
                s.then_inc(sc_done, 1)

            def turn(n):
                pe.wait_ge(a_ready, n + 1)
                transposes(TR_A + n, [atile[:, n % 2, c * P:(c + 1) * P] for c in range(4)])

            def weigh(n):
                h, tb = units[n]
                pe.wait_ge(tr_free, TR_A + n + 1)
                if n >= 2:
                    pe.wait_ge(o_free, n - 1)
                for c in range(TB):
                    o = pe.matmul(obk[:, n % 2, 0:P], aT[:, n % 2, c * P:(c + 1) * P], dv[:, c, h * P:(h + 1) * P],
                                  start=(c == 0), stop=(c == TB - 1))
                o.then_inc(o_done, 1)

            scores(0)
            for n in range(1, len(units) + 2):
                if n < len(units):
                    scores(n)
                if n >= 2:
                    turn(n - 2)
                if n >= 3:
                    weigh(n - 3)
            weigh(len(units) - 1)

            pe.wait_ge(sc_exp, len(units))

            def ret_scores(h):
                q = slice(QK * (h % 2), QK * (h % 2) + QK)
                for j in range(TB):
                    if h:
                        pe.wait_ge(rp_ready, TB * (h - 1) + j + 1)
                    pe.matmul(proj[:, j, :], rqkT[q, 2 + h // 2, j * P:(j + 1) * P], rqkT[q, h // 2, :],
                              start=True, stop=True).then_inc(rs_done, 1)

            def ret_values(h):
                n = len(units) + h
                pe.wait_ge(rp_ready, TB * (h + 1))
                pe.wait_ge(o_free, n - 1)
                for i in range(TB):
                    for j in range(TB):
                        o = pe.matmul(obk[:, n % 2, i * P:(i + 1) * P], rP[:, h % 2, j, i * P:(i + 1) * P],
                                      rv[:, j, h * P:(h + 1) * P], start=(j == 0), stop=(j == TB - 1))
                o.then_inc(o_done, 1)

            for h in range(H + 1):
                if h < H:
                    ret_scores(h)
                if h:
                    ret_values(h - 1)
            norm_transposes(TR_MIX, xn, mix_ready, 1, 0)
            pe.wait_ge(tr_free, TR_MIX + 8)
            token_major(S_OUT1, N_OUT1, hT)

            def route(layer, first):
                all_read(first)
                pe.wait_ge(in_keys, 16 * (layer + 1))
                with pe.Fori(0, N_WQ // PAIR) as it:
                    pair = it + first // PAIR

                    def key_scores(g):
                        pe.wait_ge(mm_free, pair * 8 + (g + 1 + 4))
                        pe.wait_ge(key_free, it * 8 + (layer * HP + g + 1))
                        bank = tps if g % 4 < 2 else obk
                        for tb in range(TB):
                            s = pe.matmul(bank[:, g % 2, tb * P:(tb + 1) * P], qT[:, g % 4, tb * P:(tb + 1) * P],
                                          keys(it, g), start=True, stop=True)
                        s.then_inc(key_done, 1)

                    for g in range(8):
                        if g % 4 == 0:
                            slab_landed(g // 4, pair)
                        bank_free(pair * 8 + g)
                        transposed_tile(g // 4, g % 4, hT)
                        if g:
                            key_scores(g - 1)
                    key_scores(7)

            def keys(it, g):
                return subk[:, bass.ds(it * 8 + g, 1), :].rearrange("p g n -> p (g n)")

            def clear_sum(start):
                for c in range(2 * (TB - GB)):
                    z = pe.matmul(proj[:, c, :], zeros[0:1, 0:P], zeros[0:1, P:P + 512], start=start,
                                  stop=not start, skip_group_check=True)
                return z

            def modulation(n):
                k = (S_ADA + n) % PAIR
                pe.wait_ge(slab[k], 16 * ((S_ADA + n) // PAIR + 1))
                if n >= 4:
                    pe.wait_ge(mm_free, 4 * (S_ADA + n - 3) + 4)
                for c in range(DC):
                    pe.matmul(proj[0:1, n % 4, :], silc[:, c:c + 1], wring[:, k, c * 512:(c + 1) * 512],
                              start=(c == 0), stop=False)
                pe.matmul(proj[0:1, n % 4, :], ident[0:1, 0:1], ada_row[:, n * 512:(n + 1) * 512],
                          start=False, stop=True).then_inc(mm_done, 4)

            def spread_group(grp, k, hot2_count=None):
                pe.wait_ge(hot_ready, grp + 1)
                if hot2_count is not None:
                    pe.wait_ge(hot2_ready, hot2_count)
                pe.wait_ge(spread_free, grp + 1)
                for t in range(SG):
                    m = pe.matmul(tps[:, k, t * CK:(t + 1) * CK], hot2[:, k, t, :], hot1[:, k, t, :], start=True, stop=True)
                m.then_inc(spread_done, 1)

            def experts(layer, first, job):
                all_read(first)
                def first_dots(j, k, chunks=range(DC)):
                    for c in chunks:
                        at = j * D + c * P
                        m = pe.matmul(proj[:, j, 0:DT], wring[:, k, at:at + P], hT[:, c, GB * P:T],
                                      start=(c == 0), stop=(c == DC - 1))
                    if c == DC - 1:
                        m.then_inc(mm_done, 1)

                pe.wait_ge(key_free, layer * HP + HP + 4)
                pe.wait_ge(choice_set, layer + 1)
                for b in range(TB - GB):
                    transposes(job + b, [choice[:, b, c, :] for c in range(3)])
                pe.wait_ge(tr_free, job + 2)
                with pe.Fori(0, ROUNDS) as it:
                    for g in range(RGROUPS):
                        j, half = divmod(g, 2)
                        if g % 8 == 0:
                            slab_landed(j // 4, it + first // PAIR)
                        if half == 0:
                            pe.wait_ge(z_act, it * RTILES + (layer * TILES + j + 1))
                        first_dots(j % 4, j // 4, range(half * DC // 2, (half + 1) * DC // 2))
                        spread_group(it * RGROUPS + (layer * CHUNKS * SGROUPS + g), g % 2,
                                     it * (RGROUPS // 2) + (layer * HOT2 + g // 2 + 1) if g % 2 else None)

                def spread_step(it, c, j):
                    if c < CHUNKS:
                        for g in range(2 * j, 2 * j + 2):
                            n = it * 2 * BODY + g
                            spread_group(n + (layer * CHUNKS + c) * SGROUPS, g % 2,
                                         n + (layer * HOT2 + ROUNDS * RGROUPS // 2 + (c - 1) * SGROUPS + 1))

                def dots_tile(tile, j):
                    k, at = j // 2, (j % 2) * 2 * D
                    pe.wait_ge(z_act, tile + (layer * TILES - 1 + 4))
                    for c in range(DC):
                        m = pe.matmul(obk[:, j % 2, 0:DT], wring[:, k, at + c * P:at + (c + 1) * P], hT[:, c, GB * P:T],
                                      start=(c == 0), stop=(c == DC - 1))
                    m.then_inc(z_done, 1)

                def sum_tile(tile, j, k, at, jobs):
                    pe.wait_ge(coef_t_ready, tile + (layer * TILES + 1 + 2))
                    for b in range(TB - GB):
                        for c in range(2):
                            m = pe.matmul(proj[:, 2 * b + c, :], coef_t[:, j % 2, b * P:(b + 1) * P],
                                          wring[:, k, at + c * 512:at + (c + 1) * 512],
                                          start=False, stop=False, skip_group_check=True)
                    m.then_inc(mm_done, jobs)

                pe.wait_ge(z_act, layer * TILES + CK + 4)
                clear_sum(True)
                with pe.Fori(0, STEPS // PAIR) as it:
                    for k in range(PAIR):
                        slab_landed(k, it + (first + CK // BODY) // PAIR)
                        for j in range(BODY):
                            sum_tile(it * PAIR * BODY + (k * BODY + j), j, k, j * D, 1)
                            spread_step(it * PAIR + k, 1, j)
                slab_landed(0, (first + 2 * CK // BODY) // PAIR)
                dots_tile(CK, 0)
                for c in range(1, CHUNKS):
                    def step(it, last):
                        pair = it + (first + 2 * CK // BODY) // PAIR + (c - 1) * STEPS
                        for j in range(BODY):
                            if j == 1:
                                slab_landed(1, pair)
                            if j == BODY - 1 and not last:
                                slab_landed(0, pair + 1)
                            if j < BODY - 1 or not last:
                                dots_tile(it * BODY + (c * CK + j + 1), (j + 1) % BODY)
                            spread_step(it, c + 1, j)
                            sum_tile(it * BODY + (c * CK + j), j, j // 2, (j % 2) * 2 * D + D, 2)

                    ends = c + 1 == CHUNKS
                    with pe.Fori(0, STEPS - ends) as it:
                        step(it, False)
                    if ends:
                        step(STEPS - 1, True)
                clear_sum(False).then_inc(acc_done, 1)

            norm_transposes(TR_F1, xn, xn_ready, TB, 1)
            pe.wait_ge(tr_free, TR_F1 + 8)
            route(0, S_WQ1)
            pe.wait_ge(c_silu, 1)
            pe.wait_ge(in_bias, 16)
            all_read(S_ADA)
            for n in range(N_ADA):
                modulation(n)
            experts(0, S_EXP1, TR_T1)

            norm_transposes(TR_N2, xn, xn_ready, 2 * TB, 1)
            pe.wait_ge(tr_free, TR_N2 + 8)
            all_read(S_CONV)
            transposed(S_CONV, N_CONV, hT)
            all_read(S_QK2)
            transposed(S_QK2, N_QK, hT)
            all_read(S_V2)
            token_major(S_V2, N_V, hT)
            pe.wait_ge(in_lstm, 16 * 4)
            for g in range(2):
                for c in range(DC):
                    m = pe.matmul(obk[0:MH, g, :], wif[:, c, g * MH:(g + 1) * MH], hT[:, c, :],
                                  start=(c == 0), stop=(c == DC - 1))
            m.then_inc(if_done, 1)

            pe.wait_ge(rows_ready, 1)
            for g, r in enumerate((2, 4)):
                for b in range(TB):
                    t = pe.transpose(tps[:, g, b * MH:(b + 1) * MH], mrow[0:MH, r, b * P:(b + 1) * P], ident[0:MH, 0:MH])
            t.then_inc(cols_done, 1)
            pe.wait_ge(cols_ready, 2)
            all_read(S_O2)
            pe.wait_ge(qk_ready, 8)
            pe.wait_ge(v_ones, 1)

            def gate_rows(h):
                if h >= 2:
                    pe.wait_ge(w_arg, TB * (h - 1))
                pe.matmul(tps[:, h % 2, :], sel[0:MH, h, :], mrow[0:MH, 3, :], start=True, stop=True).then_inc(nm_done, 1)

            def lstm_scores(h):
                q = slice(QK * (h % 2), QK * (h % 2) + QK)
                for s in range(TB):
                    if h:
                        pe.wait_ge(p_ready, TB * (h - 1) + s + 1)
                    pe.matmul(proj[:, s, s * P:T], kT2[q, h // 2, s * P:(s + 1) * P], qT2[q, h // 2, s * P:T],
                              start=True, stop=True).then_inc(rs_done, 1)

            def lstm_values(h):
                pe.wait_ge(p_ready, TB * (h + 1))
                if h:
                    pe.wait_ge(num_free, h)
                for b in range(TB):
                    for s in range(b + 1):
                        at = sum(T - P * u for u in range(s)) + (b - s) * P
                        m = pe.matmul(obk[:, b // 2, (b % 2) * 256:(b % 2) * 256 + P + 1], mP[:, h % 2, at:at + P],
                                      vaug[:, s, h, :], start=(s == 0), stop=(s == b))
                m.then_inc(num_done, 1)

            for h in range(MH + 1):
                if h < MH:
                    gate_rows(h)
                    lstm_scores(h)
                if h:
                    lstm_values(h - 1)
            pe.wait_ge(num_free, MH)
            token_major(S_O2, N_O, hT)
            pe.wait_ge(ym_part, N_O * TB)
            for tb in range(TB):
                for k in range(2):
                    transposes(TR_YM + 2 * tb + k, [hmw[:, tb, (4 * k + c) * P:(4 * k + c + 1) * P] for c in range(4)])
            pe.wait_ge(tr_free, TR_YM + 8)
            all_read(S_BR)
            with pe.Fori(0, N_BR // PAIR) as it:
                pair = it + S_BR // PAIR
                for k in range(PAIR):
                    slab_landed(k, pair)
                    for j, rhs in enumerate((hT, yaT, hT, ymT)):
                        bank_free(pair * 8 + (4 * k + j))
                        transposed_tile(k, j, rhs)
            all_read(S_OUT2)
            pe.wait_ge(mixT_ready, DC)
            token_major(S_OUT2, N_OUT2, mixT)
            norm_transposes(TR_F2, xn, xn_ready, 3 * TB, 1)
            pe.wait_ge(tr_free, TR_F2 + 8)
            route(1, S_WQ2)
            experts(1, S_EXP2, TR_T2)

        @block.scalar
        def _(act):
            steps = Count(act, act_s)
            for t, n in ((gain1, "attn_norm_g"),):
                act.dma_start(t, d[n]).then_inc(in_g1, 16)
            for t, n in ((ident[:, :], "ident"), (iota[:, :], "iota")):
                act.dma_start(t, d[n]).then_inc(in_cst, 16)
            for t, n in ((rope, "rope"), (part(work, 5120, 2 * NTOE), "dist"), (diffg, "diff_norm_g"),
                         (retg, "ret_norm_g"), (lamp, "diff_lambda"), (rdec, "ret_log_decay"), (ccol, "c_2"),
                         (gain2, "ffn_norm_g")):
                act.dma_start(t, d[n]).then_inc(in_blk1, 16)

            def root(dst, src, n, done):
                act.activation(dst, src, ACT.Sqrt, bias=epsc, scale=1.0 / n).then_inc(done, 1)

            def rms(src, ready):
                for tb in range(TB):
                    ready(tb)
                    steps.inc(act.activation(xn[:, tb, :], src[:, tb, :], ACT.Square, accum_out=ss[:, tb:tb + 1]))
                steps.wait()
                root(rstd, ss, D, rms_done)

            def turned(job, n, dst):
                for j in range(n):
                    act.wait_ge(tr_done, job + j + 1)
                    act.activation(dst(j), tps[:, (job + j) % 2, :].rearrange("p (c t) -> p c t", c=4),
                                   ACT.Copy).then_inc(tr_free, 1)

            def norm_turned(job, t):
                turned(job, 2 * TB, lambda j: t[:, 4 * (j % 2):4 * (j % 2) + 4, (j // 2) * P:(j // 2 + 1) * P])

            def take(s, tb, dst, func):
                act.wait_ge(mm_done, 4 * s + tb + 1)
                act.activation(dst, proj[:, tb, :], func).then_inc(mm_free, 1)

            act.wait_ge(zeros_set, 1)
            rms(x_res, lambda tb: act.wait_ge(in_x, 16))
            norm_turned(TR_N1, hT)

            for tb in range(TB):
                take(0, tb, stg[:, 0, tb, :], ACT.Copy)
            for tb in range(TB):
                take(1, tb, stg[:, 1, tb, :], ACT.Copy)
            for tb in range(TB):
                take(2, tb, dv[:, tb, :], ACT.Copy)
            turned(TR_QK, 4, lambda j: dqT[:, :, j * P:(j + 1) * P])
            for tb in range(TB):
                take(3, tb, stg[:, 0, tb, :], ACT.Copy)
            turned(TR_QK + 4, 4, lambda j: dkT[:, :, j * P:(j + 1) * P])
            for tb in range(TB):
                take(4, tb, rv[:, tb, :], ACT.Copy)
            for tb in range(TB):
                take(5, tb, rg[:, tb, :], ACT.Silu)
            turned(TR_QK + 8, 4, lambda j: rqkT[:, :, j * P:(j + 1) * P])

            act.wait_ge(lam_arg, 1)
            act.activation(lam[:, 2:4], lam[:, 0:2], ACT.Exp).then_inc(lam_exp, 1)
            act.activation(lgam, rdec, ACT.Exp).then_inc(lam_exp, 1)
            for h in range(H):
                act.wait_ge(dec_arg, h + 1)
                act.activation(decay[:, h, :], decay[:, h, :], ACT.Exp).then_inc(dec_done, 1)

            def exps(n):
                act.wait_ge(sc_max, n + 1)
                if n >= 2:
                    act.wait_ge(a_ready, n - 1)
                for m in range(2):
                    e = act.activation(prob[:, n % 2, m, :], proj[:, 2 * (n % 2) + m, :], ACT.Exp,
                                       bias=nmx[:, n % 2, m:m + 1], scale=QK ** -0.5, accum_out=psum[:, n % 2, m:m + 1])
                e.then_inc(sc_exp, 1)

            def a_turned(n):
                act.wait_ge(tr_done, TR_A + n + 1)
                if n >= 2:
                    act.wait_ge(o_done, n - 1)
                act.activation(aT[:, n % 2, :], tps[:, (TR_A + n) % 2, :], ACT.Copy).then_inc(tr_free, 1)

            def o_taken(n):
                h, tb = divmod(n, TB)
                act.wait_ge(o_done, n + 1)
                act.activation(xn[:, tb, h * P:(h + 1) * P], obk[:, n % 2, 0:P], ACT.Copy).then_inc(o_free, 1)

            for n in range(H * TB + 3):
                if n < H * TB:
                    exps(n)
                if 2 <= n < H * TB + 2:
                    a_turned(n - 2)
                if n >= 3:
                    o_taken(n - 3)
            for h in range(H):
                n = H * TB + h
                act.wait_ge(o_done, n + 1)
                act.activation(xn[:, :, 512 + h * P:512 + (h + 1) * P],
                               obk[:, n % 2, :].rearrange("p (b n) -> p b n", b=TB), ACT.Copy).then_inc(o_free, 1)
            act.wait_ge(hn_arg, 1)
            root(st16, st16, P, hn_done)
            act.wait_ge(hn_arg, 2)
            root(sv16, sv16, P, hn_done)
            norm_turned(TR_MIX, hT)
            act.activation(silc, ccol, ACT.Silu).then_inc(c_silu, 1)

            def route(layer, first):
                with act.Fori(0, N_WQ // PAIR) as it:
                    for g in range(8):
                        act.wait_ge(mm_done, it * 8 + (4 * first + g + 1))
                        act.wait_ge(key_done, it * 8 + (layer * HP + g + 1))
                        act.activation(qT[:, g % 4, :], proj[:, g % 4, :], ACT.Copy).then_inc(mm_free, 1)

            def gates(layer, tb):
                act.wait_ge(g_arg, layer * TB + tb + 1)
                act.activation(expg, expg, ACT.Exp).then_inc(g_exp, 1)

            def row_gelu(layer, u, h, func, n=GROUP):
                act.wait_ge(dot_done, u * RING + (layer * GB * SLOTS + h * GROUP + n))
                act.activation(gelu[:, h * GROUP:h * GROUP + n], dots[:, h * GROUP:h * GROUP + n], func).then_inc(gelu_done, 1)

            def spread_take(layer, c, g, k, token):
                act.wait_ge(spread_done, g + ((layer * CHUNKS + c) * SGROUPS + 1 + 2))
                act.activation(spread[:, c % 2, bass.ds(token, SG), :], tps[:, k, 0:SG * CK].rearrange("p (t n) -> p t n", t=SG),
                               ACT.Copy).then_inc(spread_free, 1)

            def hot2_group(layer, c, g, k, token, count):
                act.wait_ge(spread_done, g + ((layer * CHUNKS + c) * SGROUPS + 1))
                for t in range(SG):
                    i = act.activation(hot2[:, k, t, :], iota[:, :], ACT.Abs, bias=table[:, 3, bass.ds(token + t, 1)])
                i.then_inc(away_set, 1)
                act.wait_ge(away_set, count)
                act.activation(hot2[:, k, :, :], hot2[:, k, :, :], ACT.Relu, bias=1.0, scale=-1.0).then_inc(hot2_ready, 1)

            def tile_gelu(layer, tile, j, func):
                act.wait_ge(z_done, tile + (layer * (TILES - CK) + 1 - CK))
                act.wait_ge(coef_t_ready, tile + (layer * TILES + 1))
                act.activation(act_z[:, j % 2, :], obk[:, j % 2, 0:DT], func).then_inc(z_act, 1)

            def modulation(n):
                act.wait_ge(mm_done, 4 * (S_ADA + n + 1))
                act.activation(ada_row[:, n * 512:(n + 1) * 512], proj[0:1, n % 4, :], ACT.Copy).then_inc(mm_free, 4)

            def store_modulation():
                act.wait_ge(mm_free, 4 * S_EXP1 + 4)
                act.dma_start(ada_dram, ada_row).then_inc(ada_stored, 16)
                act.wait_ge(ada_stored, 16)

            def ada(first, n):
                return ada_dram[0:1, first * D:(first + n) * D].to_broadcast([P, n * D])

            def experts(layer, first, job, func):
                def first_gelu(t, j):
                    act.wait_ge(mm_done, t + (4 * first + 1))
                    act.activation(first_z[:, bass.ds(t, 1), :].rearrange("p i t -> p (i t)"), proj[:, j, 0:DT],
                                   func).then_inc(z_act, 1)

                def modulations(stage):
                    n = N_ADA // (GB + 1)
                    if layer == 0 and stage <= GB:
                        for m in range(stage * n, (stage + 1) * n):
                            modulation(m)
                        if stage == GB:
                            store_modulation()

                for b in range(GB):
                    modulations(b)
                    gates(layer, b)
                for u in range(ROUTED):
                    row_gelu(layer, u, 0, func)
                    gates(layer, GB + u)
                    row_gelu(layer, u, 1, func)
                    modulations(GB + u)
                for b in range(TB - GB):
                    act.wait_ge(tr_done, job + b + 1)
                    bank = tps[:, (job + b) % 2, :].rearrange("p (c t) -> p c t", c=4)
                    act.activation(table[:, 0:3, b * P:(b + 1) * P], bank[:, 0:3, :], ACT.Copy)
                    act.activation(table[:, 3, b * P:(b + 1) * P], bank[:, 1, :], ACT.Copy, scale=-1.0).then_inc(tr_free, 1)
                act.wait_ge(tr_free, job + 2)
                with act.Fori(0, ROUNDS) as it:
                    for g in range(RGROUPS):
                        j, k = divmod(g, 2)
                        token = it * (RGROUPS * SG) + g * SG
                        if k == 0:
                            hot2_group(layer, 0, it * RGROUPS + (g + 1), 1, token + SG,
                                       it * (RGROUPS // 2) + (layer * HOT2 + j + 1))
                        else:
                            first_gelu(it * RTILES + j, j % 4)
                        spread_take(layer, 0, it * RGROUPS + g, k, token)
                        if g % 4 == 1:
                            row_gelu(layer, it * 2 + (ROUTED + g // 8), g // 4 % 2, func)
                for c in range(CHUNKS):
                    if c:
                        act.wait_ge(coef_t_ready, layer * TILES + c * CK + 2)
                    if c + 1 == CHUNKS:
                        late_loads(layer)
                    with act.Fori(0, STEPS) as it:
                        for j in range(BODY):
                            gs = range(2 * j, 2 * j + 2) if c + 1 < CHUNKS else ()
                            if c:
                                tile_gelu(layer, it * BODY + (c * CK + j), j, func)
                            for g in gs:
                                n = it * 2 * BODY + g
                                hot2_group(layer, c + 1, n, g % 2, it * (2 * BODY * SG) + g * SG,
                                           n + (layer * HOT2 + ROUNDS * RGROUPS // 2 + c * SGROUPS + 1))
                            if j % 2 == 0:
                                row_gelu(layer, it + (EARLY + c * STEPS), j // 2, func)
                            if c == 0:
                                act.wait_ge(coef_t_ready, it * BODY + (layer * TILES + j + 1 + 2))
                            for g in gs:
                                spread_take(layer, c + 1, it * 2 * BODY + g, g % 2, it * (2 * BODY * SG) + g * SG)
                row_gelu(layer, UNITS, 0, func, TAIL)

            def late_loads(layer):
                if layer == 0:
                    act.dma_start(late[:, 0, :], d["final_norm_g"]).then_inc(in_late, 16)
                    act.dma_start(late[:, 1, :], d["norm1_pre_2"]).then_inc(in_late, 16)
                    act.dma_start(mod1, ada(0, 2).rearrange("p (k n) -> p k n", k=2)).then_inc(in_mod1, 16)
                else:
                    act.dma_start(late[:, 0, :], ada(5, 1)).then_inc(in_last, 16)
                    act.dma_start(late[:, 1, :], d["norm2_post_2"]).then_inc(in_last, 16)

            rms(x_res, lambda tb: act.wait_ge(mm_free, 4 * (S_OUT1 + 1) + tb + 1 + 4))
            norm_turned(TR_F1, hT)
            act.dma_start(subk, d["keys1"]).then_inc(in_keys, 16)
            act.dma_start(ada_row, d["b_ada_2"]).then_inc(in_bias, 16)
            route(0, S_WQ1)
            experts(0, S_EXP1, TR_T1, ACT.Gelu)

            rms(x_res, lambda tb: act.wait_ge(acc_free, tb + 1) if tb < GB else
                act.wait_ge(mm_free, 4 * S_EXP1 + 4 * N_EXP // (TB - GB) * (tb - GB + 1) + 4))
            rms(x_res, lambda tb: act.wait_ge(x_ready, tb + 1))
            act.dma_start(convw, d["conv_w"]).then_inc(in_conv, 16)
            act.dma_start(mod2, ada(2, 3).rearrange("p (k n) -> p k n", k=3)).then_inc(in_mod2, 16)
            for t, n in ((tri[:, :], "tri"), (bif, "b_if"), (wif, "w_if"), (sel[0:MH, :, :], "sel")):
                act.dma_start(t, d[n]).then_inc(in_lstm, 16)
            norm_turned(TR_N2, hT)
            for j in range(DC):
                job = 4 * S_CONV + 3 * j
                act.wait_ge(mm_done, job + 1)
                if j >= 2:
                    act.wait_ge(mm_free, job - 3 + 4)
                act.activation(csb[:, j % 2, :], proj[:, job % 4, :], ACT.Copy).then_inc(c_copied, 1)
            act.wait_ge(mm_free, 4 * S_QK2 + 4)
            act.wait_ge(qk_conv, 1)

            def qk_silu(j):
                act.wait_ge(qk_conv, j + 2)
                act.activation((qT2 if j < 4 else kT2)[:, j % 4, :], ctmp[:, j % 2, :], ACT.Silu).then_inc(qk_ready, 1)

            for j in range(N_QK * 4):
                act.wait_ge(mm_done, 4 * S_QK2 + j + 1)
                if j >= 2:
                    act.wait_ge(qk_conv, j)
                act.activation(cx[:, j % 2, 3:3 + T], proj[:, j % 4, :], ACT.Copy).then_inc(mm_free, 1)
                if j:
                    qk_silu(j - 1)
            qk_silu(N_QK * 4 - 1)
            for s in range(N_V):
                for tb in range(TB):
                    act.wait_ge(mm_done, 4 * (S_V2 + s) + tb + 1)
                    act.activation(vaug[:, tb, 4 * s:4 * s + 4, 0:P], proj[:, tb, :].rearrange("p (h n) -> p h n", h=4),
                                   ACT.Copy).then_inc(mm_free, 1)

            act.wait_ge(if_act, 1)
            steps.inc(act.activation(mrow[0:MH, 0, :], mrow[0:MH, 1, :], ACT.Abs))
            steps.wait()
            steps.inc(act.activation(mrow[0:MH, 0, :], mrow[0:MH, 0, :], ACT.Exp, scale=-1.0))
            steps.wait()
            act.activation(mrow[0:MH, 0, :], mrow[0:MH, 0, :], ACT.Ln, bias=1.0).then_inc(ln_done, 1)
            act.wait_ge(if_act, 2)
            act.activation(mrow[0:MH, 4, :], mrow[0:MH, 4, :], ACT.Exp, scale=-1.0).then_inc(rows_ready, 1)
            act.dma_start(mhg, d["mh_norm_w_2"]).then_inc(in_mhg, 16)
            act.wait_ge(cols_done, 1)
            for g, t in enumerate((acol, ecol)):
                act.activation(t, tps[:, g, 0:TB * MH].rearrange("p (b h) -> p b h", b=TB),
                               ACT.Copy).then_inc(cols_ready, 1)
            for n in range(MH * TB):
                s = n % TB
                act.wait_ge(w_arg, n + 1)
                act.activation(wts[:, n % 2, s * P:T], wts[:, n % 2, s * P:T], ACT.Exp).then_inc(w_exp, 1)
            act.wait_ge(hn_arg, 3)
            root(st32, st32, P, hn_done)
            for n in range(N_O * TB):
                act.wait_ge(mm_done, 4 * S_O2 + n + 1)
                if n >= 4:
                    act.wait_ge(ym_part, n - 3)
                act.activation(sig[:, n % 4, :], proj[:, n % 4, :], ACT.Sigmoid).then_inc(mm_free, 1)
            norm_turned(TR_YM, ymT)
            for n in range(2 * DC):
                act.wait_ge(mm_done, 4 * S_BR + 2 * n + 1)
                if n >= 4:
                    act.wait_ge(mixT_ready, (n - 4) // 2 + 1)
                act.activation(sig[:, n % 4, :], proj[:, (2 * n) % 4, :], ACT.Sigmoid).then_inc(g_sig, 1)
            act.wait_ge(mixT_ready, DC)
            for k, n in enumerate(("norm1_post_2", "norm2_pre_2")):
                act.dma_start(post[:, k, :], d[n]).then_inc(in_post, 16)
            act.dma_start(subk, d["keys2"]).then_inc(in_keys, 16)
            for s in range(N_OUT2):
                for tb in range(TB):
                    take(S_OUT2 + s, tb, hmw[:, tb, s * 512:(s + 1) * 512], ACT.Copy)
            act.wait_ge(mm_free, 4 * S_WQ2 + 4)
            rms(hmw, lambda tb: None)
            rms(x_res, lambda tb: act.wait_ge(x_ready, TB + tb + 1))
            norm_turned(TR_F2, hT)
            route(1, S_WQ2)
            experts(1, S_EXP2, TR_T2, ACT.Gelu_apprx_tanh)
            act.wait_ge(slot_free, 2 * GB * SLOTS + RING)
            act.wait_ge(acc_done, 2)
            for tb in range(TB):
                steps.inc(act.activation(out_row(tb), peer_sum(tb), ACT.Square, accum_out=ss[:, tb:tb + 1]))
                steps.wait()
                root(rstd[:, tb:tb + 1], ss[:, tb:tb + 1], D, rms_done)

        @block.vector
        def _(v):
            steps = Count(v, vec)

            def link(ins):
                steps.inc(ins)
                steps.wait()

            def bcast(t, axis, shape):
                return t.unsqueeze(axis).to_broadcast(shape)

            v.memset(epsc, EPS).then_inc(vec, 1)
            steps.n += 1
            for k, (s, n) in enumerate(((mm_free, 4), (key_done, 4), (key_free, 4), (slot_free, RING), (spread_done, 2),
                                        (spread_free, 2), (z_act, 4), (coef_t_ready, 2))):
                v.memset(zeros[:, 80 * k:80 * (k + 1)], 0.0).then_inc(s, n)
            v.memset(dots[:, :], 0.0).then_inc(zeros_set, 1)

            def inverse_rms(n):
                v.wait_ge(rms_done, n)
                link(v.reciprocal(rstd, rstd))

            v.wait_ge(in_g1, 16)
            inverse_rms(1)
            for tb in range(TB):
                v.scalar_tensor_tensor(xn[:, tb, :], x_res[:, tb, :], rstd[:, tb:tb + 1], gain1,
                                       ALU.mult, ALU.mult).then_inc(xn_ready, 1)

            def rotate(n, s, src, half, cos, sin):
                v.wait_ge(mm_free, 4 * (s + 1) + 4)
                x = stg[:, src, :, :].rearrange("p b (h e) -> p b h e", e=QK)
                x1, x2 = x[:, :, :, 0:half], x[:, :, :, half:2 * half]
                shape = [P, TB, 8, half]
                t = [rtmp[:, k, 0:TB * 8 * half].rearrange("p (b h e) -> p b h e", b=TB, h=8) for k in range(4)]
                c, s_ = bcast(cos, 2, shape), bcast(sin, 2, shape)
                for k, (a, b) in enumerate(((x1, c), (x2, s_), (x2, c), (x1, s_))):
                    i = v.tensor_tensor(t[k], a, b, ALU.mult)
                link(i)
                v.tensor_tensor(x1, t[0], t[1], ALU.subtract)
                v.tensor_tensor(x2, t[2], t[3], ALU.add).then_inc(rotated, 1)
                v.wait_ge(rotated, n + 1)

            v.wait_ge(in_blk1, 16 * 8)
            rotate(0, 0, 0, 8, cosd, sind)
            rotate(1, 1, 1, 8, cosd, sind)
            rotate(2, 3, 0, 32, cosr, sinr)

            for m in range(2):
                i = v.scalar_tensor_tensor(rtmp[:, m, 0:QK], lamp[:, 2 * m * QK:(2 * m + 1) * QK], 1.0,
                                           lamp[:, (2 * m + 1) * QK:(2 * m + 2) * QK], ALU.mult, ALU.mult,
                                           accum_out=lam[:, m:m + 1])
                if m:
                    i.then_inc(lam_arg, 1)
            v.wait_ge(lam_exp, 2)
            v.scalar_tensor_tensor(lam[:, 0:1], lam[:, 3:4], LAMBDA_INIT, lam[:, 2:3], ALU.subtract, ALU.subtract)
            link(v.tensor_scalar(lgam, lgam, -1.0, None, ALU.mult))
            for h in range(H):
                link(v.tensor_scalar(decay[:, h, :], dist[:, 0, :], lgam[:, h:h + 1], None, ALU.mult))
                v.scalar_tensor_tensor(decay[:, h, :], dist[:, 1, :], lgam[:, H + h:H + h + 1], decay[:, h, :],
                                       ALU.mult, ALU.add).then_inc(dec_arg, 1)

            def maxima(n):
                v.wait_ge(sc_done, n + 1)
                if n >= 2:
                    v.wait_ge(sc_exp, n - 1)
                link(v.tensor_reduce(mx[:, n % 2, :], proj[:, 2 * (n % 2):2 * (n % 2) + 2, :], AX, ALU.max))
                v.tensor_scalar(nmx[:, n % 2, :], mx[:, n % 2, :], -QK ** -0.5, None, ALU.mult).then_inc(sc_max, 1)

            def mixed(n):
                k = n % 2
                v.wait_ge(sc_exp, n + 1)
                link(v.reciprocal(pinv[:, k, :], psum[:, k, :]))
                link(v.tensor_scalar(pinv[:, k, 1:2], pinv[:, k, 1:2], lam[:, 0:1], None, ALU.mult))
                if n >= 2:
                    v.wait_ge(tr_done, TR_A + n - 1)
                link(v.tensor_scalar(atile[:, k, :], prob[:, k, 0, :], pinv[:, k, 0:1], None, ALU.mult))
                v.scalar_tensor_tensor(atile[:, k, :], prob[:, k, 1, :], pinv[:, k, 1:2], atile[:, k, :],
                                       ALU.mult, ALU.add).then_inc(a_ready, 1)

            for n in range(H * TB + 1):
                if n < H * TB:
                    maxima(n)
                if n:
                    mixed(n - 1)

            for h in range(H):
                v.wait_ge(dec_done, h + 1)
                if h >= 2:
                    v.wait_ge(o_done, H * TB + h - 1)
                for j in range(TB):
                    v.wait_ge(rs_done, TB * h + j + 1)
                    at = (TB - 1 - j) * P
                    v.scalar_tensor_tensor(rP[:, h % 2, j, :], proj[:, j, :], QK ** -0.5, decay[:, h, at:at + T],
                                           ALU.mult, ALU.mult).then_inc(rp_ready, 1)

            full = [P, TB, H, P]
            a = xn[:, :, 0:512].rearrange("p b (h n) -> p b h n", h=H)
            r = xn[:, :, 512:1024].rearrange("p b (h n) -> p b h n", h=H)
            v.wait_ge(o_free, H * TB)
            link(v.tensor_tensor(sq16, a, a, ALU.mult))
            v.tensor_reduce(st16, sq16, AX, ALU.add).then_inc(hn_arg, 1)
            v.wait_ge(hn_done, 1)
            link(v.reciprocal(st16, st16))
            link(v.tensor_scalar(st16, st16, 1.0 - LAMBDA_INIT, None, ALU.mult))
            link(v.tensor_tensor(a, a, bcast(st16, 3, full), ALU.mult))
            link(v.tensor_tensor(a, a, diffg.unsqueeze(1).unsqueeze(1).to_broadcast(full), ALU.mult))
            v.wait_ge(o_free, H * TB + H)
            link(v.tensor_reduce(st16, r, AX, ALU.add))
            link(v.tensor_scalar(st16, st16, 1.0 / P, None, ALU.mult))
            link(v.tensor_tensor(r, r, bcast(st16, 3, full), ALU.subtract))
            link(v.tensor_tensor(sq16, r, r, ALU.mult))
            v.tensor_reduce(sv16, sq16, AX, ALU.add).then_inc(hn_arg, 1)
            v.wait_ge(hn_done, 2)
            link(v.reciprocal(sv16, sv16))
            link(v.tensor_tensor(r, r, bcast(sv16, 3, full), ALU.mult))
            link(v.tensor_tensor(xn[:, :, 512:1024], xn[:, :, 512:1024], bcast(retg, 1, [P, TB, 512]), ALU.mult))
            v.tensor_tensor(xn[:, :, 512:1024], xn[:, :, 512:1024], rg, ALU.mult).then_inc(mix_ready, 1)

            for s in range(N_OUT1):
                for tb in range(TB):
                    v.wait_ge(mm_done, 4 * (S_OUT1 + s) + tb + 1)
                    c = slice(512 * s, 512 * (s + 1))
                    v.tensor_tensor(x_res[:, tb, c], x_res[:, tb, c], proj[:, tb, :], ALU.add).then_inc(mm_free, 1)
            inverse_rms(2)
            for tb in range(TB):
                v.scalar_tensor_tensor(xn[:, tb, :], x_res[:, tb, :], rstd[:, tb:tb + 1], gain2,
                                       ALU.mult, ALU.mult).then_inc(xn_ready, 1)

            LOW = -3.0e38

            def rank_keys(layer):
                for g in range(HP):
                    bank = tps if g % 4 < 2 else obk
                    s = [bank[:, g % 2, tb * P:(tb + 1) * P] for tb in range(TB)]
                    v.wait_ge(key_done, layer * HP + g + 1 + 4)
                    for tb in range(TB):
                        i = v.max(tops[:, tb, g, 0:8], s[tb])
                    link(i)
                    for tb in range(TB):
                        v.max_index(topu[:, tb, g, 0:8], tops[:, tb, g, 0:8], s[tb])
                    for tb in range(TB):
                        i = v.match_replace(srep[:, g % 2, tb, :], tops[:, tb, g, 0:8], s[tb], LOW)
                    i.then_inc(key_free, 1)
                    v.wait_ge(key_free, layer * HP + g + 1 + 4)
                    for tb in range(TB):
                        i = v.max(tops[:, tb, g, 8:16], srep[:, g % 2, tb, :])
                    link(i)
                    for tb in range(TB):
                        i = v.max_index(topu[:, tb, g, 8:16], tops[:, tb, g, 8:16], srep[:, g % 2, tb, :])
                link(i)
                link(v.tensor_copy(topi, topu))

            grid = [P, PH, K, K]

            def choose(layer, tb):
                s = tops[:, tb, :, :].rearrange("p (h c) k -> p h c k", c=2)
                c = cand
                for i0, i1, n in ((0, LONG, K), (LONG, K, SHORT)):
                    box = [P, PH, i1 - i0, n]
                    at = 0 if i0 == 0 else LONG * K
                    i = v.tensor_tensor(c[:, :, at:at + (i1 - i0) * n].rearrange("p h (i j) -> p h i j", j=n),
                                        bcast(s[:, :, 0, i0:i1], 3, box), bcast(s[:, :, 1, 0:n], 2, box), ALU.add)
                link(i)
                for h in range(PH):
                    i = v.max(best[:, h, 0:8], c[:, h, :])
                link(i)
                for h in range(PH):
                    v.max_index(posu[:, h, 0:8], best[:, h, 0:8], c[:, h, :])
                for h in range(PH):
                    i = v.match_replace(cand2[:, h, :], best[:, h, 0:8], c[:, h, :], LOW)
                link(i)
                for h in range(PH):
                    i = v.max(best[:, h, 8:16], cand2[:, h, :])
                link(i)
                for h in range(PH):
                    i = v.max_index(posu[:, h, 8:16], best[:, h, 8:16], cand2[:, h, :])
                link(i)
                v.tensor_single_scalar(half_u, posu, 2, ALU.logical_shift_right)
                link(v.tensor_copy(half_f, posu))
                link(v.tensor_copy(pos_row, half_u))
                link(v.tensor_scalar(pos_row, pos_row, float(K - SHORT), float(-(K - SHORT) * LONG * K // SHORT), ALU.mult, ALU.add))
                link(v.scalar_tensor_tensor(posu, pos_row, 0.0, half_f, ALU.max, ALU.add))
                v.tensor_tensor(expg, best, best[:, :, 0:1].to_broadcast([P, PH, K]), ALU.subtract).then_inc(g_arg, 1)
                v.wait_ge(g_arg, layer * TB + tb + 1)

            def key_numbers(tb, m):
                ids = topi[:, tb, :, :].rearrange("p (h c) k -> p h c k", c=2)
                op, arg = ((ALU.logical_shift_right, 4), (ALU.bitwise_and, 15))[m]
                link(v.tensor_single_scalar(half_u, posu, arg, op))
                link(v.tensor_copy(half_f, half_u))
                link(v.tensor_tensor(onehot, bcast(half_f, 3, grid), iota[:, 0:K].unsqueeze(1).unsqueeze(1).to_broadcast(grid),
                                     ALU.is_equal))
                link(v.tensor_tensor(onehot, onehot, bcast(ids[:, :, m, :], 2, grid), ALU.mult))
                link(v.tensor_reduce(idf[:, m, :, :] if tb < GB else by_head(choice[:, tb - GB, m, :]), onehot, AX, ALU.add))

            def by_head(t):
                return t.rearrange("p (h k) -> p h k", h=PH)

            def chosen(layer, tb):
                if tb < GB:
                    v.scalar_tensor_tensor(by_head(eid[:, :, tb]), idf[:, 0, :, :], float(NK), idf[:, 1, :, :],
                                           ALU.mult, ALU.add).then_inc(eid_ready, 1)
                v.wait_ge(g_exp, layer * TB + tb + 1)
                link(v.tensor_reduce(gsum, expg, AX, ALU.add))
                link(v.reciprocal(gsum, gsum))
                g = by_head(gate[:, :, tb] if tb < GB else choice[:, tb - GB, 2, :])
                i = v.tensor_tensor(g, expg, bcast(gsum, 2, [P, PH, K]), ALU.mult)
                if tb + 1 == TB:
                    i.then_inc(choice_set, 1)
                else:
                    link(i)

            def row_dots(layer, u, h, n=GROUP, first=0):
                for r in range(h * GROUP + first, h * GROUP + n):
                    v.wait_ge(row[r], u * 16 + 16 * (layer * (UNITS + (r < TAIL)) + 1))
                    v.scalar_tensor_tensor(rows[:, r, 0:D], rows[:, r, 0:D], 1.0, xn[:, r % GB, :], ALU.mult, ALU.mult,
                                           accum_out=dots[:, r:r + 1]).then_inc(dot_done, 1)

            def row_coefs(layer, u, h, n=GROUP):
                at = slice(h * GROUP, h * GROUP + n)
                v.wait_ge(gelu_done, u * 2 + (layer * GROUPS + h + 1))
                v.tensor_tensor(coef[:, at], gelu[:, at],
                                gate[:, :, :].rearrange("p s b -> p (s b)")[:, bass.ds(u * RING + h * GROUP, n)],
                                ALU.mult).then_inc(coef_done, 1)

            def row_sums(layer, u, h, n=GROUP, first=0):
                v.wait_ge(coef_done, u * 2 + (layer * GROUPS + h + 1))
                for r in range(h * GROUP + first, h * GROUP + n):
                    v.wait_ge(slot_free, u * RING + (layer * GB * SLOTS + r - 1 + RING))
                    v.scalar_tensor_tensor(gathered[:, r % GB, :], rows[:, r, D:2 * D], coef[:, r:r + 1], gathered[:, r % GB, :],
                                           ALU.mult, ALU.add).then_inc(slot_free, 1)

            def hot_group(layer, c, g, k, token, both=False):
                first = (layer * CHUNKS + c) * SGROUPS
                tok = bass.ds(token, SG)
                v.wait_ge(spread_done, g + (first + 1))
                v.tensor_tensor(hot1[:, k, :, :], iota[:, c * CK:(c + 1) * CK].unsqueeze(1).to_broadcast([P, SG, CK]),
                                bcast(table[:, 0, tok], 2, [P, SG, CK]), ALU.is_equal).then_inc(hot1_set, 1)
                if both:
                    v.tensor_tensor(hot2[:, k, :, :], iota[:, :].unsqueeze(1).to_broadcast([P, SG, NK]),
                                    bcast(table[:, 1, tok], 2, [P, SG, NK]), ALU.is_equal)
                v.wait_ge(hot1_set, g + (first + 1))
                v.tensor_tensor(hot1[:, k, :, :], hot1[:, k, :, :], bcast(table[:, 2, tok], 2, [P, SG, CK]),
                                ALU.mult).then_inc(hot_ready, 1)

            def tile_coefs(layer, first, c, key, j):
                tile = key + c * CK
                v.wait_ge(z_act, tile + (layer * TILES + 1 + 4))
                v.wait_ge(mm_done, tile + (4 * first + CK - 1) if c == 0 else tile * 2 + (4 * first - 2))
                z = first_z[:, bass.ds(key, 1), :].rearrange("p i t -> p (i t)") if c == 0 else act_z[:, j % 2, :]
                v.tensor_tensor(coef_t[:, j % 2, :], z,
                                spread[:, c % 2, :, bass.ds(key, 1)].rearrange("p t n -> p (t n)"),
                                ALU.mult).then_inc(coef_t_ready, 1)

            def experts(layer, first, job):
                rank_keys(layer)
                v.wait_ge(tr_free, job)
                link(v.memset(gathered, 0.0))
                for tb in range(GB):
                    choose(layer, tb)
                    key_numbers(tb, 0)
                    key_numbers(tb, 1)
                    chosen(layer, tb)
                for u in range(ROUTED):
                    row_dots(layer, u, 0)
                    choose(layer, GB + u)
                    row_coefs(layer, u, 0)
                    row_dots(layer, u, 1)
                    key_numbers(GB + u, 0)
                    row_sums(layer, u, 0)
                    row_coefs(layer, u, 1)
                    key_numbers(GB + u, 1)
                    chosen(layer, GB + u)
                    row_sums(layer, u, 1)
                v.wait_ge(tr_free, job + 2)
                with v.Fori(0, ROUNDS) as it:
                    for g in range(RGROUPS):
                        hot_group(layer, 0, it * RGROUPS + g, g % 2, it * (RGROUPS * SG) + g * SG, g % 2 == 0)
                        u, h = it * 2 + (ROUTED + g // 8), g // 4 % 2
                        if g % 4 == 0:
                            row_dots(layer, u, h, 2)
                        elif g % 4 == 1:
                            row_dots(layer, u, h, 3, 2)
                        elif g % 4 == 2:
                            row_coefs(layer, u, h)
                            row_sums(layer, u, h, 1)
                        else:
                            row_sums(layer, u, h, 3, 1)
                for c in range(CHUNKS):
                    v.wait_ge(spread_free, (layer * CHUNKS + c + 1) * SGROUPS + 2)
                    if c == 1:
                        v.wait_ge(mm_done, 4 * first + 2 * CK - 1)
                    with v.Fori(0, STEPS) as it:
                        u = it + (EARLY + c * STEPS)
                        for j in range(BODY):
                            if c == 0:
                                tile_coefs(layer, first, c, it * BODY + j, j)
                            elif j % 2 == 0:
                                row_dots(layer, u, j // 2)
                            if c + 1 < CHUNKS:
                                for g in range(2 * j, 2 * j + 2):
                                    hot_group(layer, c + 1, it * 2 * BODY + g, g % 2, it * (2 * BODY * SG) + g * SG)
                            if c:
                                tile_coefs(layer, first, c, it * BODY + j, j)
                            elif j % 2 == 0:
                                row_dots(layer, u, j // 2)
                            if j % 2 == (c == 0):
                                row_coefs(layer, u, j // 2)
                            if j % 2:
                                row_sums(layer, u, j // 2)
                row_dots(layer, UNITS, 0, TAIL)
                row_coefs(layer, UNITS, 0, TAIL)
                row_sums(layer, UNITS, 0, TAIL)
                v.wait_ge(slot_free, (layer + 1) * GB * SLOTS + RING)

            experts(0, S_EXP1, TR_T1)
            for tb in range(TB):
                if tb == GB:
                    v.wait_ge(acc_done, 1)
                x = x_res[:, tb, :].rearrange("p (k n) -> p k n", k=2)
                i = v.tensor_tensor(x, x, peer_sum(tb), ALU.add)
                if tb < GB:
                    i.then_inc(acc_free, 1)
                else:
                    i.then_inc(mm_free, 4 * N_EXP // (TB - GB))

            v.wait_ge(in_late, 32)
            inverse_rms(3)
            for tb in range(TB):
                v.scalar_tensor_tensor(x_res[:, tb, :], x_res[:, tb, :], rstd[:, tb:tb + 1], late[:, 0, :],
                                       ALU.mult, ALU.mult).then_inc(x_ready, 1)
            v.wait_ge(in_mod1, 16)
            link(v.scalar_tensor_tensor(mod1[:, 1, :], mod1[:, 1, :], 1.0, late[:, 1, :], ALU.add, ALU.mult))

            def modulated(scale, shift):
                for tb in range(TB):
                    link(v.scalar_tensor_tensor(xn[:, tb, :], x_res[:, tb, :], rstd[:, tb:tb + 1], scale,
                                                ALU.mult, ALU.mult))
                    v.tensor_tensor(xn[:, tb, :], xn[:, tb, :], shift, ALU.add).then_inc(xn_ready, 1)

            inverse_rms(4)
            modulated(mod1[:, 1, :], mod1[:, 0, :])

            link(v.memset(cx[:, :, 0:2], 0.0))
            v.wait_ge(in_conv, 16)
            for j in range(DC):
                job, k = 4 * S_CONV + 3 * j, j % 2
                v.wait_ge(c_copied, j + 1)
                v.wait_ge(mm_done, job + 2)
                v.tensor_tensor(cx[:, k, 2:2 + T], csb[:, k, :], proj[:, (job + 1) % 4, :], ALU.mult).then_inc(mm_free, 2)
                v.wait_ge(mm_free, job + 2 + 4)
                link(v.tensor_scalar(ctmp[:, k, :], cx[:, k, 0:T], convw[:, 3 * j:3 * j + 1], None, ALU.mult))
                for t in (1, 2):
                    link(v.scalar_tensor_tensor(ctmp[:, k, :], cx[:, k, t:t + T], convw[:, 3 * j + t:3 * j + t + 1],
                                                ctmp[:, k, :], ALU.mult, ALU.add))
                v.wait_ge(mm_done, job + 3)
                v.tensor_tensor(yaT[:, j, :], ctmp[:, k, :], proj[:, (job + 2) % 4, :], ALU.mult).then_inc(mm_free, 1)

            v.wait_ge(mm_free, 4 * S_QK2 + 4)
            v.memset(cx[:, :, 0:3], 0.0).then_inc(qk_conv, 1)
            for j in range(N_QK * 4):
                k, w = j % 2, 24 + 4 * j
                v.wait_ge(mm_free, 4 * S_QK2 + j + 1 + 4)
                if j >= 2:
                    v.wait_ge(qk_ready, j - 1)
                link(v.tensor_scalar(ctmp[:, k, :], cx[:, k, 0:T], convw[:, w:w + 1], None, ALU.mult))
                for t in (1, 2, 3):
                    i = v.scalar_tensor_tensor(ctmp[:, k, :], cx[:, k, t:t + T], convw[:, w + t:w + t + 1],
                                               ctmp[:, k, :], ALU.mult, ALU.add)
                    if t < 3:
                        link(i)
                    else:
                        i.then_inc(qk_conv, 1)
            v.memset(vaug[:, :, :, P:P + 1], 1.0).then_inc(v_ones, 1)

            v.wait_ge(in_lstm, 16 * 4)
            v.wait_ge(if_done, 1)
            g = [mrow[0:MH, k, :] for k in range(5)]
            v.tensor_scalar(g[2], obk[0:MH, 0, :], bif[:, 0:1], None, ALU.add)
            link(v.tensor_scalar(g[1], obk[0:MH, 1, :], bif[:, 1:2], None, ALU.add))
            v.memset(dots[:, :], 0.0).then_inc(if_act, 1)
            v.wait_ge(ln_done, 1)
            link(v.scalar_tensor_tensor(g[1], g[1], 0.0, g[0], ALU.min, ALU.subtract))
            link(v.memset(g[0], 1.0))
            link(v.tensor_tensor_scan(g[4], g[0], g[1], 0.0, ALU.mult, ALU.add))
            link(v.tensor_tensor(g[2], g[2], g[4], ALU.subtract))
            link(v.tensor_tensor_scan(g[3], g[2], g[2], 0.0, ALU.max, ALU.max))
            link(v.tensor_tensor(g[4], g[4], g[3], ALU.add))
            v.tensor_scalar(g[3], g[3], -1.0, None, ALU.mult).then_inc(if_act, 1)

            def weight_arg(n):
                h, s = divmod(n, TB)
                v.wait_ge(nm_done, h + 1)
                if n >= 2:
                    v.wait_ge(p_ready, n - 1)
                v.tensor_scalar(wts[:, n % 2, s * P:T], tps[:, h % 2, s * P:T], acol[:, s, h:h + 1], 0.0,
                                ALU.add, ALU.min).then_inc(w_arg, 1)

            def weighted(n):
                h, s = divmod(n, TB)
                at = sum(T - P * u for u in range(s))
                if h >= 2 and s == 0:
                    v.wait_ge(num_done, h - 1)
                v.wait_ge(rs_done, H * TB + n + 1)
                v.wait_ge(w_exp, n + 1)
                link(v.scalar_tensor_tensor(mP[:, h % 2, at:at + T - s * P], proj[:, s, s * P:T], QK ** -0.5,
                                            wts[:, n % 2, s * P:T], ALU.mult, ALU.mult))
                dg = mP[:, h % 2, at:at + P]
                v.tensor_tensor(dg, dg, tri[:, :], ALU.mult).then_inc(p_ready, 1)

            nums = obk[:, :, :].rearrange("p k (e n) -> p (k e) n", e=2)

            def head_out(h):
                v.wait_ge(num_done, h + 1)
                dn = nums[:, :, P:P + 1].rearrange("p b n -> p (b n)")
                link(v.tensor_scalar(den, dn, -1.0, None, ALU.mult))
                link(v.tensor_tensor(den, den, dn, ALU.max))
                link(v.tensor_tensor(den, den, ecol[:, :, h], ALU.max))
                link(v.reciprocal(dinv, den))
                v.tensor_tensor(hm[:, :, h, :], nums[:, :, 0:P], bcast(dinv, 2, [P, TB, P]), ALU.mult).then_inc(num_free, 1)

            v.wait_ge(cols_ready, 2)
            for n in range(MH * TB + 1):
                if n < MH * TB:
                    weight_arg(n)
                if n:
                    weighted(n - 1)
                    if n % TB == 0 and n > TB:
                        head_out(n // TB - 2)
            head_out(MH - 1)

            v.wait_ge(num_free, MH)
            x32 = xn[:, :, :].rearrange("p b (h n) -> p b h n", h=MH)
            link(v.tensor_tensor(x32, hm, hm, ALU.mult))
            v.tensor_reduce(st32, x32, AX, ALU.add).then_inc(hn_arg, 1)
            v.wait_ge(hn_done, 3)
            link(v.reciprocal(st32, st32))
            link(v.tensor_tensor(hm, hm, bcast(st32, 3, [P, TB, MH, P]), ALU.mult))
            v.wait_ge(in_mhg, 16)
            link(v.tensor_tensor(hmw, hmw, bcast(mhg, 1, [P, TB, D]), ALU.mult))
            for n in range(N_O * TB):
                s, tb = divmod(n, TB)
                c = slice(512 * s, 512 * (s + 1))
                v.wait_ge(mm_free, 4 * S_O2 + n + 1 + 4)
                v.tensor_tensor(hmw[:, tb, c], hmw[:, tb, c], sig[:, n % 4, :], ALU.mult).then_inc(ym_part, 1)

            for n in range(2 * DC):
                j, m = divmod(n, 2)
                v.wait_ge(g_sig, n + 1)
                v.wait_ge(mm_done, 4 * S_BR + 2 * n + 2)
                if n >= 4:
                    v.wait_ge(mixT_ready, (n - 4) // 2 + 1)
                v.tensor_tensor(sig[:, n % 4, :] if m else br1[:, j % 2, :], sig[:, n % 4, :], proj[:, (2 * n + 1) % 4, :],
                                ALU.mult).then_inc(mm_free, 2)
                if m:
                    v.wait_ge(mm_free, 4 * S_BR + 2 * n + 2 + 4)
                    v.tensor_tensor(mixT[:, j, :], br1[:, j % 2, :], sig[:, n % 4, :], ALU.add).then_inc(mixT_ready, 1)

            v.wait_ge(in_post, 16 * 2)
            v.wait_ge(in_mod2, 16)
            v.tensor_tensor(mod2[:, 0, :], mod2[:, 0, :], post[:, 0, :], ALU.mult)
            link(v.scalar_tensor_tensor(mod2[:, 2, :], mod2[:, 2, :], 1.0, post[:, 1, :], ALU.add, ALU.mult))
            inverse_rms(5)
            for tb in range(TB):
                link(v.scalar_tensor_tensor(hmw[:, tb, :], hmw[:, tb, :], rstd[:, tb:tb + 1], mod2[:, 0, :], ALU.mult, ALU.mult))
                v.tensor_tensor(x_res[:, tb, :], x_res[:, tb, :], hmw[:, tb, :], ALU.add).then_inc(x_ready, 1)
            inverse_rms(6)
            modulated(mod2[:, 2, :], mod2[:, 1, :])

            experts(1, S_EXP2, TR_T2)
            v.wait_ge(in_last, 16 * 2)
            link(v.tensor_tensor(late[:, 0, :], late[:, 0, :], late[:, 1, :], ALU.mult))
            for tb in range(TB):
                v.wait_ge(rms_done, 7 + tb)
                link(v.reciprocal(rstd[:, tb:tb + 1], rstd[:, tb:tb + 1]))
                link(v.scalar_tensor_tensor(out_row(tb), peer_sum(tb), rstd[:, tb:tb + 1],
                                            late[:, 0, :].rearrange("p (k n) -> p k n", k=2), ALU.mult, ALU.mult))
                x = x_res[:, tb, :].rearrange("p (k n) -> p k n", k=2)
                v.tensor_tensor(x, x, out_row(tb), ALU.add).then_inc(out_ready, 1)


def by_rows(w):
    return w.reshape(DC, P, -1, 512).transpose(2, 1, 0, 3).reshape(-1, P, SLAB)


def by_tiles(tiles):
    t = np.stack(tiles).reshape(-1, 4, DC, P, P)
    return t.transpose(0, 3, 1, 2, 4).reshape(-1, P, SLAB)


def by_experts(u, v):
    ut = u.reshape(NK, NK, DC, P).transpose(0, 3, 2, 1).reshape(NK, P, D)
    v = v.reshape(NK, NK, D)

    def slabs(t):
        n = SLAB // t.shape[2]
        return t.reshape(-1, n, P, t.shape[2]).transpose(0, 2, 1, 3).reshape(-1, P, SLAB)

    return np.concatenate([slabs(ut[:CK]), slabs(v[:CK]), slabs(np.concatenate([ut, v], axis=2)[CK:])])


def columns(w):
    return [w[:, c:c + P] for c in range(0, w.shape[1], P)]


def broad(a):
    return np.ascontiguousarray(np.broadcast_to(np.reshape(a, (1, -1)), (P, np.size(a))))


def constants():
    pos = np.arange(T, dtype=np.float32)
    fd = np.power(np.float32(500000.0), -np.arange(8, dtype=np.float32) * np.float32(2.0) / np.float32(16))
    fr = np.float32(1.0) / np.power(np.float32(10000.0), np.linspace(0.0, 1.0, 32, dtype=np.float32))
    rope = []
    for f in (fd, fr):
        ang = (pos[:, None] * f[None, :].astype(np.float32)).astype(np.float32)
        for fn in (np.cos, np.sin):
            rope.append(fn(ang).astype(np.float32).reshape(TB, P, -1).transpose(1, 0, 2).reshape(P, -1))
    away = np.arange(2 * T - P, dtype=np.float32)[None, :] - (T - P) - np.arange(P, dtype=np.float32)[:, None]
    sel = np.zeros((MH, MH, P), np.float32)
    sel[np.arange(MH), np.arange(MH)] = 1.0
    return {
        "rope": np.concatenate(rope, axis=1),
        "dist": np.concatenate([np.maximum(away, 0), np.maximum(-away, 0)], axis=1),
        "ident": np.eye(P, dtype=np.float32),
        "tri": np.triu(np.ones((P, P), np.float32)),
        "iota": np.ascontiguousarray(np.broadcast_to(np.arange(NK, dtype=np.float32), (P, NK))),
        "sel": sel,
    }


def lay_out(inp):
    a = {k: np.asarray(v) for k, v in inp.items()}
    w2 = a["w_in_2"][0]
    cuts = np.cumsum([1024, 1024, 1024, 512, 512, 1024, 1024, 8, 8, 1024])
    cg, bg, xi, q, k, v, o, ig, fg, ga, gm = np.split(w2, cuts, axis=1)
    conv = [t for c, x, b in zip(columns(cg), columns(xi), columns(bg)) for t in (c, x, b)]
    br = [t for g1, wa, g2, wm in zip(columns(ga), columns(a["w_branch_a_2"][0]), columns(gm), columns(a["w_branch_m_2"][0]))
          for t in (g1, wa, g2, wm)]
    slabs = np.concatenate([
        by_rows(a["w_in"][0]), by_rows(a["w_out"][0]), by_tiles(columns(a["peer_w_query"][0])), by_rows(a["w_ada_2"][0]),
        by_experts(a["peer_u"][0], a["peer_v"][0]), by_tiles(conv), by_tiles(columns(q) + columns(k)), by_rows(v), by_rows(o), by_tiles(br), by_rows(a["w_out_2"][0]),
        by_tiles(columns(a["peer_wq_2"][0])), by_experts(a["peer_u_2"][0], a["peer_v_2"][0])])
    d = constants()
    d.update(
        x=a["x"][0], slabs=slabs, c_2=np.ascontiguousarray(a["c_2"].reshape(DC, P).T),
        experts1=np.concatenate([a["peer_u"][0], a["peer_v"][0]], axis=1),
        experts2=np.concatenate([a["peer_u_2"][0], a["peer_v_2"][0]], axis=1),
        keys1=np.ascontiguousarray(a["peer_sub_keys"][0].reshape(HP, NK, P).transpose(2, 0, 1)),
        keys2=np.ascontiguousarray(a["peer_subkeys_2"][0].reshape(HP, NK, P).transpose(2, 0, 1)),
        b_ada_2=a["b_ada_2"].reshape(1, 6 * D),
        conv_w=np.ascontiguousarray(np.concatenate([
            a["conv_a_w_2"][0].reshape(3, DC, P).transpose(2, 1, 0).reshape(P, -1),
            a["conv_qk_w_2"][0].reshape(4, DC, P).transpose(2, 1, 0).reshape(P, -1)], axis=1)),
        b_if=np.ascontiguousarray(np.stack([a["b_igate_2"][0], a["b_fgate_2"][0]], axis=1)),
        w_if=np.ascontiguousarray(np.concatenate([ig, fg], axis=1).reshape(DC, P, 2 * MH).transpose(1, 0, 2)),
    )
    for n in ("attn_norm_g", "diff_norm_g", "ret_norm_g", "diff_lambda", "ret_log_decay", "ffn_norm_g", "final_norm_g",
              "norm1_pre_2", "norm1_post_2", "norm2_pre_2", "norm2_post_2", "mh_norm_w_2"):
        d[n] = broad(a[n])
    return {k: np.ascontiguousarray(t, dtype=np.float32) for k, t in d.items()}


def kernel(**inputs):
    import concourse.bacc as bacc
    from concourse.bass_utils import run_bass_kernel_spmd

    arrays = lay_out(inputs)
    nc = bacc.Bacc("TRN2", target_bir_lowering=False, num_devices=1)
    d = {n: nc.dram_tensor(f"in_{n}", t.shape, F32, kind="ExternalInput").ap() for n, t in arrays.items()}
    out = nc.dram_tensor("out", (T, D), F32, kind="ExternalOutput").ap()
    build(nc, d, out)
    got = run_bass_kernel_spmd(nc, [{f"in_{n}": t for n, t in arrays.items()}], core_ids=[0])
    return got.results[0]["out"].reshape(1, T, D)
```
